# Optimizing a Trainium2 kernel written in Bass

```python
import math
import jax, jax.numpy as jnp
from jax import lax
import numpy as np

D_MODEL = 1024
BATCH = 1
SEQ = 256
DEPTH = 2
DEC_BATCH = 8
DEC_SEQ = 8
PAST_LEN = 2048
PAGE_SIZE = 128

GM_WIDTH = 1024
GM_GROUPS = 4
GM_GROUP_DIM = GM_WIDTH // GM_GROUPS
GM_CHUNK = 128
HG_HEADS = 8
HG_DK = 128
HG_DV = 128
HG_WIDTH = HG_HEADS * HG_DK
HG_CHUNK = 64
D_FF = 2816
N_EXPERTS = 8
TOP_K = 2
D_FF_EXPERT = 2816
N_DENSE = (DEPTH + 1) // 2
N_MOE = DEPTH // 2
IN_COLS = 2 * GM_WIDTH + 4 * HG_WIDTH + 2 * D_MODEL
EPS = 1e-6

kernel_name = "hybrid_gmlp_hgrn2_decoder_step"

def _rmsnorm(x, w):
    xf = x.astype(jnp.float32)
    y = xf * lax.rsqrt(jnp.mean(xf * xf, axis=-1, keepdims=True) + EPS)
    return (y * w.astype(jnp.float32)).astype(x.dtype)

def _layernorm(x, w, b):
    xf = x.astype(jnp.float32)
    mu = jnp.mean(xf, axis=-1, keepdims=True)
    xc = xf - mu
    y = xc * lax.rsqrt(jnp.mean(xc * xc, axis=-1, keepdims=True) + EPS)
    return (y * w.astype(jnp.float32) + b.astype(jnp.float32)).astype(x.dtype)

def _lower_bounds(raw):
    p = jax.nn.softmax(raw.astype(jnp.float32), axis=0)
    c = jnp.cumsum(p, axis=0)
    return c - c[0:1]

def _spatial_gate(v, w_s, b_s):
    B, T, _ = v.shape
    L = min(T, GM_CHUNK)
    n = T // L
    mask = jnp.tril(jnp.ones((L, L), dtype=bool))
    w = jnp.where(mask[None], w_s[:, :L, :L], 0.0).astype(v.dtype)
    vc = v.reshape(B, n, L, GM_GROUPS, GM_GROUP_DIM)
    mixed = jnp.einsum('gts,bnsgc->bntgc', w, vc)
    mixed = mixed + b_s[:, :L].T.astype(v.dtype)[None, None, :, :, None]
    return mixed.reshape(B, T, GM_WIDTH)

def _hgrn2(q, logf, i, s0):
    B, T = q.shape[:2]
    C = math.gcd(T, HG_CHUNK)
    n = T // C
    k = -jnp.expm1(logf)

    def to_chunks(a):
        return a.astype(jnp.float32).reshape(B, n, C, HG_HEADS, a.shape[-1]).transpose(1, 0, 3, 2, 4)

    qc, gc, kc, ic = to_chunks(q), to_chunks(logf), to_chunks(k), to_chunks(i)
    causal = jnp.tril(jnp.ones((C, C), dtype=bool))[:, :, None]

    def step(S, xs):
        qb, gb, kb, ib = xs
        bcum = jnp.cumsum(gb, axis=2)
        diff = bcum[:, :, :, None, :] - bcum[:, :, None, :, :]
        decay = jnp.where(causal, jnp.exp(jnp.where(causal, diff, 0.0)), 0.0)
        scores = jnp.einsum('bhtk,bhtsk,bhsk->bhts', qb, decay, kb)
        o = jnp.einsum('bhts,bhsv->bhtv', scores, ib) + jnp.einsum('bhtk,bhkv->bhtv', qb * jnp.exp(bcum), S)
        btot = bcum[:, :, -1]
        kdec = kb * jnp.exp(btot[:, :, None, :] - bcum)
        S_new = jnp.exp(btot)[..., None] * S + jnp.einsum('bhsk,bhsv->bhkv', kdec, ib)
        return S_new, o

    S, o = lax.scan(step, s0.astype(jnp.float32), (qc, gc, kc, ic))
    o = o.transpose(1, 0, 3, 2, 4).reshape(B, T, HG_HEADS, HG_DV)
    return o, S

def _mixer(h, s0, lb, w_in, gm_ln_w, gm_ln_b, gm_ws, gm_bs, hg_norm_w, w_branch_a, w_branch_b, w_out):
    B, T, _ = h.shape
    z = h @ w_in
    sizes = (GM_WIDTH, GM_WIDTH, HG_WIDTH, HG_WIDTH, HG_WIDTH, HG_WIDTH, D_MODEL, D_MODEL)
    points = [sum(sizes[:j]) for j in range(1, len(sizes))]
    u, v, q, f, i, g, ga, gb = jnp.split(z, points, axis=-1)
    u = jax.nn.gelu(u, approximate=False)
    v = _layernorm(jax.nn.gelu(v, approximate=False), gm_ln_w, gm_ln_b)
    a = u * _spatial_gate(v, gm_ws, gm_bs)
    qh = jax.nn.silu(q).reshape(B, T, HG_HEADS, HG_DK)
    zf = f.astype(jnp.float32)
    logf = jnp.logaddexp(jax.nn.log_sigmoid(zf), jnp.log(lb.astype(jnp.float32)) + jax.nn.log_sigmoid(-zf))
    logf = logf.reshape(B, T, HG_HEADS, HG_DK)
    ih = i.reshape(B, T, HG_HEADS, HG_DV)
    o, s_new = _hgrn2(qh, logf, ih, s0)
    o = _rmsnorm(o, hg_norm_w).astype(h.dtype)
    o = (o * jax.nn.silu(g).reshape(B, T, HG_HEADS, HG_DV)).reshape(B, T, HG_WIDTH)
    merged = jax.nn.sigmoid(ga) * (a @ w_branch_a) + jax.nn.sigmoid(gb) * (o @ w_branch_b)
    return merged @ w_out, s_new, v

def _swiglu(h, w_gate, w_up, w_down):
    return (jax.nn.silu(h @ w_gate) * (h @ w_up)) @ w_down

def _moe(h, w_router, b_router, w_gate, w_up, w_down):
    logits = (h @ w_router).astype(jnp.float32) + b_router.astype(jnp.float32)
    top_vals, top_idx = lax.top_k(logits, TOP_K)
    wts = jax.nn.softmax(top_vals, axis=-1)
    combine = jnp.sum(jax.nn.one_hot(top_idx, N_EXPERTS, dtype=jnp.float32) * wts[..., None], axis=-2)
    combine = combine.astype(h.dtype)
    out = jnp.zeros_like(h)
    for e in range(N_EXPERTS):
        out = out + combine[..., e:e + 1] * _swiglu(h, w_gate[e], w_up[e], w_down[e])
    return out

def setup_inputs(seed: int = 0) -> dict:
    key = jax.random.key(seed)
    ks = jax.random.split(key, 40)
    nrm = lambda k, shape, s: jax.random.normal(k, shape, jnp.float32) * s
    d = D_MODEL
    return {
        "x_prompt": nrm(ks[0], (BATCH, SEQ, d), 1.0),
        "x_sample": nrm(ks[1], (DEC_BATCH, DEC_SEQ, d), 1.0),
        "c_prompt": nrm(ks[2], (BATCH, d), 1.0),
        "c_sample": nrm(ks[3], (DEC_BATCH, d), 1.0),
        "state_hgrn": nrm(ks[4], (DEPTH, DEC_BATCH, HG_HEADS, HG_DK, HG_DV), 0.5),
        "w_in": nrm(ks[5], (DEPTH, d, IN_COLS), d ** -0.5),
        "gm_ln_w": 1.0 + nrm(ks[6], (DEPTH, GM_WIDTH), 0.02),
        "gm_ln_b": nrm(ks[7], (DEPTH, GM_WIDTH), 0.02),
        "gm_ws": nrm(ks[8], (DEPTH, GM_GROUPS, GM_CHUNK, GM_CHUNK), GM_CHUNK ** -0.5),
        "gm_bs": 1.0 + nrm(ks[9], (DEPTH, GM_GROUPS, GM_CHUNK), 0.02),
        "hg_lb_raw": nrm(ks[10], (DEPTH, HG_WIDTH), 0.5),
        "hg_norm_w": 1.0 + nrm(ks[11], (DEPTH, HG_DV), 0.02),
        "w_branch_a": nrm(ks[12], (DEPTH, GM_WIDTH, d), GM_WIDTH ** -0.5),
        "w_branch_b": nrm(ks[13], (DEPTH, HG_WIDTH, d), HG_WIDTH ** -0.5),
        "w_out": nrm(ks[14], (DEPTH, d, d), d ** -0.5),
        "w_ada": nrm(ks[15], (DEPTH, d, 6 * d), 0.5 * d ** -0.5),
        "b_ada": nrm(ks[16], (DEPTH, 6 * d), 0.02),
        "norm_pre_mix": 1.0 + nrm(ks[17], (DEPTH, d), 0.02),
        "norm_post_mix": 1.0 + nrm(ks[18], (DEPTH, d), 0.02),
        "norm_pre_ffn": 1.0 + nrm(ks[19], (DEPTH, d), 0.02),
        "norm_post_ffn": 1.0 + nrm(ks[20], (DEPTH, d), 0.02),
        "w_ffn_gate": nrm(ks[21], (N_DENSE, d, D_FF), d ** -0.5),
        "w_ffn_up": nrm(ks[22], (N_DENSE, d, D_FF), d ** -0.5),
        "w_ffn_down": nrm(ks[23], (N_DENSE, D_FF, d), D_FF ** -0.5),
        "w_router": nrm(ks[24], (N_MOE, d, N_EXPERTS), d ** -0.5),
        "b_router": nrm(ks[25], (N_MOE, N_EXPERTS), 0.01),
        "w_exp_gate": nrm(ks[26], (N_MOE, N_EXPERTS, d, D_FF_EXPERT), d ** -0.5),
        "w_exp_up": nrm(ks[27], (N_MOE, N_EXPERTS, d, D_FF_EXPERT), d ** -0.5),
        "w_exp_down": nrm(ks[28], (N_MOE, N_EXPERTS, D_FF_EXPERT, d), D_FF_EXPERT ** -0.5),
    }

def reference(x_prompt, x_sample, c_prompt, c_sample, state_hgrn, w_in, gm_ln_w, gm_ln_b, gm_ws, gm_bs,
              hg_lb_raw, hg_norm_w, w_branch_a, w_branch_b, w_out, w_ada, b_ada,
              norm_pre_mix, norm_post_mix, norm_pre_ffn, norm_post_ffn,
              w_ffn_gate, w_ffn_up, w_ffn_down, w_router, b_router, w_exp_gate, w_exp_up, w_exp_down):
    lb = _lower_bounds(hg_lb_raw)

    def run_layer(x, c, s0, l):
        mod = (jax.nn.silu(c) @ w_ada[l] + b_ada[l])[:, None, :]
        sh1, sc1, g1, sh2, sc2, g2 = jnp.split(mod, 6, axis=-1)
        h = _rmsnorm(x, norm_pre_mix[l]) * (1.0 + sc1) + sh1
        mix, s_new, v_rows = _mixer(h, s0, lb[l], w_in[l], gm_ln_w[l], gm_ln_b[l], gm_ws[l], gm_bs[l],
                                    hg_norm_w[l], w_branch_a[l], w_branch_b[l], w_out[l])
        x = x + g1 * _rmsnorm(mix, norm_post_mix[l])
        h = _rmsnorm(x, norm_pre_ffn[l]) * (1.0 + sc2) + sh2
        j = l // 2
        if l % 2 == 0:
            f = _swiglu(h, w_ffn_gate[j], w_ffn_up[j], w_ffn_down[j])
        else:
            f = _moe(h, w_router[j], b_router[j], w_exp_gate[j], w_exp_up[j], w_exp_down[j])
        x = x + g2 * _rmsnorm(f, norm_post_ffn[l])
        return x, s_new, v_rows

    y_prompt, y_sample = x_prompt, x_sample
    s_prompt0 = jnp.zeros((x_prompt.shape[0], HG_HEADS, HG_DK, HG_DV), jnp.float32)
    hp, hs, vs = [], [], []
    for l in range(DEPTH):
        y_prompt, s_p, _v_p = run_layer(y_prompt, c_prompt, s_prompt0, l)
        y_sample, s_s, v_s = run_layer(y_sample, c_sample, state_hgrn[l], l)
        hp.append(s_p.astype(x_prompt.dtype))
        hs.append(s_s.astype(state_hgrn.dtype))
        vs.append(v_s)
    new_state_hgrn_prompt = jnp.stack(hp, axis=0)
    new_state_hgrn_sample = jnp.stack(hs, axis=0)
    new_gmlp_v_sample = jnp.stack(vs, axis=0)
    return (y_prompt, y_sample, new_state_hgrn_prompt, new_state_hgrn_sample, new_gmlp_v_sample)


_drawn_inputs = setup_inputs


def setup_inputs(seed=0):
    import zlib

    import numpy as np

    out = dict(_drawn_inputs(seed))
    spreads = {}
    factors = {'gm_ln_w': 7.736,
     'gm_ln_b': 8.885,
     'gm_bs': 10.394,
     'hg_norm_w': 3.793,
     'norm_post_mix': 2.731,
     'norm_post_ffn': 3.095,
     'b_router': 2.852}
    for name, (base, spread) in spreads.items():
        noise = np.random.default_rng([zlib.crc32(name.encode()), seed]).standard_normal(out[name].shape)
        drawn = base * np.exp(spread * noise) if base else spread * noise
        out[name] = __import__('jax').numpy.asarray(drawn.astype(out[name].dtype))
    for name, factor in factors.items():
        out[name] = (out[name] * factor).astype(out[name].dtype)
    return out
```

```python
from contextlib import ExitStack

import numpy as np

import concourse.bass as bass
from concourse import mybir

F32 = mybir.dt.float32
F32R = mybir.dt.float32r
I32 = mybir.dt.int32
U8 = mybir.dt.uint8
U32 = mybir.dt.uint32
ALU = mybir.AluOpType
ACT = mybir.ActivationFunctionType
AX = mybir.AxisListType

P = 128
D = 1024
KD = D // P
TP = 256
NS, LS = 8, 8
TS = NS * LS
T = TP + TS
SEQS = 1 + NS
TT = 3
HEADS = 8
G4 = 4
FF = 2816
KF = FF // P
NE = 8
DEPTH = 2
EPS = 1e-6
CW = 256
LEVELS = [1, 2, 4, 8, 16, 32, 64]
ADA_TILES = 6 * KD
EXTRA = 4
JOBS = NE + EXTRA
JCH = 33
JAUX = 24

PARTS = ["f", "q", "i", "v", "u", "g", "A", "ga", "gb", "B", "O"]
COL = {"u": 0, "v": 1024, "q": 2048, "f": 3072, "i": 4096, "g": 5120, "ga": 6144, "gb": 7168}
BASE = {}
for _l in range(DEPTH):
    for _n, _p in enumerate(PARTS):
        BASE[_l, _p] = _l * 82 + 4 * _n
GU_BASE, DOWN_BASE = 44, 66
CHUNKS = 82 + 44
ADA_FIRST = 2 * KD

C_ID, C_IOTA, C_TRI, C_UPPER, C_SEQ, C_IOTA8, C_N = 0, 128, 256, 384, 512, 520, 528


def constants():
    c = np.zeros((P, C_N), np.float32)
    i = np.arange(P)
    c[:, C_ID:C_ID + P] = np.eye(P)
    c[:, C_IOTA:C_IOTA + P] = i[None, :]
    c[:, C_TRI:C_TRI + P] = i[:, None] < i[None, :]
    c[:, C_UPPER:C_UPPER + P] = i[:, None] <= i[None, :]
    c[:TS, C_SEQ:C_SEQ + NS] = i[:TS, None] // LS == np.arange(NS)[None, :]
    c[:, C_IOTA8:C_IOTA8 + 8] = np.arange(8)[None, :]
    m = np.zeros((P, 1 + len(LEVELS), P), np.float32)
    m[:, 0] = np.eye(P)
    s, t = i[:, None], i[None, :]
    for n, b in enumerate(LEVELS):
        m[:, n + 1] = (s // (2 * b) == t // (2 * b)) & (s // b % 2 == 0) & (t // b % 2 == 1)
    return c, m


class Seen:

    def __init__(self, eng):
        self.eng, self.n = eng, {}

    def next(self, sem):
        self.n[id(sem)] = self.n.get(id(sem), 0) + 1
        self.eng.wait_ge(sem, self.n[id(sem)])

    def step(self, ins, sem):
        ins.then_inc(sem, 1)
        self.next(sem)


def build(nc, a, out):
    ctx = ExitStack()
    with ctx:
        sems = {}

        def sem(name):
            if name not in sems:
                sems[name] = ctx.enter_context(nc.semaphore(name))
            return sems[name]

        low = (nc.sbuf_base + 31) // 32 * 32

        def at(name, shape, dt, offset):
            return nc.alloc_sbuf_tensor_at(name, shape, dt, offset=low + offset, align_bytes=16)

        RING = 0
        O_X = 73728
        O_H1 = O_X + 10240
        HLB = 4 * (KD * T + 64)
        O_H2 = O_H1 + 2 * HLB
        O_F = O_H2 + 2 * HLB
        O_Q = O_F + 12288
        O_K = O_Q + 10240
        O_I = O_K + 10240
        O_V = O_I + 12288
        O_A = O_V + 12288
        O_M = O_A + 10240
        RAW = at("raw", [P, 2, KD * CW], F32, RING)
        WHI = at("whi", [P, 2, KD * CW], F32R, RING + 16384)
        WLO = at("wlo", [P, 2, KD * CW], F32R, RING + 32768)
        ADA = at("ada", [P, 2, KD, P], F32, RING + 49152)
        SC = at("sc", [P, 2560], F32, RING + 57344)
        WST = at("wst", [P, G4, P], F32, RING + 67584)
        WSS = at("wss", [TS, G4, TS], F32, RING + 69632)
        T2 = at("t2", [P, 2, T], F32, RING + 70656)
        MRAW = at("mraw", [P, 3, KD * CW], F32, RING)
        MHI = at("mhi", [P, 3, KD * CW], F32R, RING + 24576)
        MLO = at("mlo", [P, 3, KD * CW], F32R, RING + 49152)
        X = at("x", [P, KD, T], F32, O_X)
        H1H = at("h1h", [P, KD * T + 64], F32R, O_H1)
        H1L = at("h1l", [P, KD * T + 64], F32R, O_H1 + HLB)
        H2H = at("h2h", [P, KD * T + 64], F32R, O_H2)
        H2L = at("h2l", [P, KD * T + 64], F32R, O_H2 + HLB)
        LNW = at("lnw", [P, D], F32, O_H2)
        LNB = at("lnb", [P, D], F32, O_H2 + 4096)
        WSR = at("wsr", [P, G4, P], F32, O_H2 + 8192)
        WSRS = at("wsrs", [TS, G4, TS], F32, O_H2 + HLB)
        GB = at("gb", [P, KD, T], F32, O_H2 + HLB)
        SQ = at("sq", [P, KD, T], F32, O_F)
        FG = at("fg", [P, HEADS, T], F32, O_F)
        KTM = at("ktm", [P, TT, D], F32, O_F)
        OT = at("ot", [P, 512], F32, O_F)
        OSQ = at("osq", [P, 512], F32, O_F + 2048)
        ON = at("on", [P, 512], F32, O_F + 4096)
        HT = at("ht", [P, KD, T], F32, O_Q)
        QQ = at("qq", [P, HEADS, T], F32, O_Q)
        KK = at("kk", [P, HEADS, T], F32, O_K)
        ST = at("st", [P, 2, HEADS, P], F32, O_K)
        IT = at("it", [P, TT, D], F32, O_I)
        VT = at("vt", [P, TT, D], F32, O_V)
        GS = at("gs", [P, KD, T], F32, O_V)
        SA = at("sa", [P, KD, T], F32, O_A)
        BA = at("ba", [P, 1280], F32, O_A)
        BB = at("bb", [P, 640], F32, O_A + 5120)
        IM = at("im", [TS, 2, D], F32, RING + 57344)
        PRH = at("prh", [P, KF, T], F32R, O_F)
        PRL = at("prl", [P, KF, T], F32R, O_F + 4 * KF * T)
        XTM = at("xtm", [P, TT, D], F32, O_I)
        CT = at("ct", [SEQS, D], F32, O_Q)
        VR = at("vr", [P, 2, P], F32, O_K)
        HMH = at("hmh", [P, TT, D], F32R, O_H1)
        HML = at("hml", [P, TT, D], F32R, O_H1 + 12288)
        XEH = at("xeh", [P, KD, P], F32R, O_H1 + 24576)
        XEL = at("xel", [P, KD, P], F32R, O_H1 + 28672)
        PM = at("pm", [P, TT, P], F32R, O_H1 + 32768)
        PW = at("pw", [P, TT, P], F32, O_H1 + 34304)
        PTS = at("pts", [P, T], F32, O_H1 + 35840)
        YE = at("ye", [P, D], F32, O_H1 + 37120)
        SG = at("sg", [P, FF], F32, O_F)
        GTH = at("gth", [P, KF, P], F32R, O_F + 11264)
        GTL = at("gtl", [P, KF, P], F32R, O_F + 22528)
        WR = at("wr", [P, KD, NE], F32, O_V)
        BR = at("br", [P, NE], F32, O_V + 256)
        R0 = O_V + 512
        LG = at("lg", [P, TT, NE], F32, R0)
        TOPV = at("topv", [P, TT, 8], F32, R0 + 96)
        TOPI = at("topi", [P, TT, 8], U32, R0 + 192)
        TOPF = at("topf", [P, TT, 2], F32, R0 + 288)
        S1 = at("s1", [P, TT, NE], F32, R0 + 320)
        S2 = at("s2", [P, TT, NE], F32, R0 + 416)
        SEL = at("sel", [P, TT, NE], F32, R0 + 512)
        WT = at("wt", [P, TT, NE], F32, R0 + 608)
        PR = at("pr", [P, TT, 4], F32, R0 + 704)
        POS = at("pos", [P, TT, NE], F32, R0 + 768)
        CNT = at("cnt", [P, 8, NE], F32, R0 + 864)
        POSJ = at("posj", [P, TT, JOBS + 1], F32, R0 + 1184)
        WJ = at("wj", [P, TT, JOBS + 1], F32, R0 + 1376)
        OH = at("oh", [P, 3, NE], F32, R0 + 1568)
        JT = at("jt", [P, TT, NE], F32, R0 + 1696)
        XI = at("xi", [1, 8], I32, R0 + 1824)
        XF = at("xf", [P, 8], F32, R0 + 1856)
        o = O_M
        CF = at("cf", [P, C_N], F32, o)
        CM = at("cm", [P, 8, P], U8, o + 2112)
        ONES = at("ones", [P, P], F32, o + 3136)
        MOD = at("mod", [P, 2 * ADA_TILES, SEQS], F32, o + 3648)
        VEC = at("vec", [P, 2, P], F32, o + 7104)
        CS = at("cs", [P, KD, SEQS], F32, o + 8128)
        RST = at("rst", [P, 512], F32, o + 8416)
        RSTD = at("rstd", [P, 512], F32, o + 10464)
        AM = at("am", [P, KD, SEQS], F32, o + 12512)
        LB = at("lb", [P, DEPTH, KD], F32, o + 12800)
        OML = at("oml", [P, DEPTH, KD], F32, o + 12864)
        LT = at("lt", [P, 3, KD], F32, o + 12928)
        BP = at("bp", [P, HEADS, 2], F32, o + 13024)
        BS = at("bs", [P, HEADS, NS], F32, o + 13088)
        BN = at("bn", [P, TT, 12], F32, o + 13344)
        MV = at("mv", [P, TT, 4], F32, o + 13488)
        T1 = at("t1", [P, 2, 2, T], F32, o + 13536)
        BGS = at("bgs", [P, T], F32, O_A + 7680)
        assert low + o + 18656 <= nc.sbuf_usable_end, (low + o + 18656, nc.sbuf_usable_end)

        PS = ctx.enter_context(nc.psum_tensor("ps", [P, 8, 512], F32))
        ident = CF[:, C_ID:C_ID + P]

        wide = {}
        for l in range(DEPTH):
            for p in PARTS:
                src = {"A": a["w_branch_a"], "B": a["w_branch_b"], "O": a["w_out"]}.get(p, a["w_in"])
                wide[l, p] = (src[l].rearrange("(k p) n -> p k n", p=P), COL.get(p, 0))
        ada_src = [a["w_ada"][l].rearrange("(k p) n -> p k n", p=P) for l in range(DEPTH)]
        gate_src = a["w_ffn_gate"][0].rearrange("(k p) n -> p k n", p=P)
        up_src = a["w_ffn_up"][0].rearrange("(k p) n -> p k n", p=P)
        down_src = a["w_ffn_down"][0].rearrange("(k p) n -> p k n", p=P)

        raw_in = [sem("raw_in0"), sem("raw_in1")]
        hi_made, lo_made = sem("hi_made"), sem("lo_made")
        chunk_used = sem("chunk_used")
        psum_out = sem("psum_out")
        ada_in = [sem("ada_in0"), sem("ada_in1")]
        ada_used, ada_made = sem("ada_used"), sem("ada_made")
        aux_in, aux_out = sem("aux_in"), sem("aux_out")
        sq_made, stat_in, ms_made, std_made = sem("sq_made"), sem("stat_in"), sem("ms_made"), sem("std_made")
        dve_step = sem("dve_step")
        act_step = sem("act_step")
        x_ready = sem("x_ready")
        operand = sem("operand")
        m_raw = [sem(f"m_raw{n}") for n in range(3)]
        m_hi, m_lo, m_used = sem("m_hi"), sem("m_lo"), sem("m_used")
        gate_out, prod_made, y_made = sem("gate_out"), sem("prod_made"), sem("y_made")
        m_aux_in, m_aux_out, p_made, gt_hi = sem("m_aux_in"), sem("m_aux_out"), sem("p_made"), sem("gt_hi")

        def through(eng, base, n, body, loop=True):
            if loop and base:
                with eng.Fori(0, n // 2) as i:
                    for j in range(2):
                        body(i * 2 + (base + j), i + base // 2, j, i * 2 + j)
            else:
                for k in range(n):
                    body(base + k, (base + k) // 2, k % 2, k)

        def hm_unit(t, k, number):
            n = P if k < 4 else TS
            return t[0:n, k // 2, 512 * (k % 2):512 * (k % 2) + 512], PS[0:n, 4 + number % 2, :]

        def states_stored(eng, l):
            eng.wait_ge(sem("sp_stored"), 16 * (l + 1))
            eng.wait_ge(sem("st_stored0"), 16 * 4 * (l + 1))
            eng.wait_ge(sem("st_stored1"), 16 * 4 * (l + 1))

        mark = {}

        block = ctx.enter_context(nc.Block())

        @block.sync
        def _(sp):
            def load_raw(c, j, src, cols=KD * CW):
                if not (isinstance(c, int) and c < 2):
                    sp.wait_ge(lo_made, c - 1)
                sp.dma_start(RAW[:, j, 0:cols].rearrange("p (k n) -> p k n", k=src.shape[1]),
                             src).then_inc(raw_in[j], 16)

            def load_ada(t, j, l, col):
                if not (isinstance(t, int) and t < 2):
                    sp.wait_ge(ada_used, t - 1)
                sp.dma_start(ADA[:, j], ada_src[l][:, :, bass.ds(col, P)]).then_inc(ada_in[j], 16)

            for t in range(ADA_FIRST):
                load_ada(t, t % 2, 0, t * P)
                if t in (4, 8):
                    src, c0 = wide[0, "f"]
                    n = t // 4 - 1
                    load_raw(n, n, src[:, :, c0 + n * CW:c0 + (n + 1) * CW])

            for l in range(DEPTH):
                for p in PARTS:
                    src, c0 = wide[l, p]
                    base = BASE[l, p]

                    def one(c, r, j, n):
                        if not (isinstance(c, int) and c < 2):
                            load_raw(c, j, src[:, :, bass.ds(n * CW + c0, CW)])
                        if l == 0:
                            al, first = (0, ADA_FIRST + base) if base < 32 else (1, base - 32)
                            load_ada(c + ADA_FIRST, j, al, (n + first) * P)
                    through(sp, base, 4, one, loop=(base > 0))
                if l == 0:
                    with sp.Fori(0, 11) as i:
                        for j, src in enumerate((gate_src, up_src)):
                            load_raw(i * 2 + (GU_BASE + j), j, src[:, :, bass.ds(i * CW, CW)])
                            load_ada(i * 2 + (GU_BASE + j + ADA_FIRST), j, 1, (i * 2 + (12 + j)) * P)
                    def down(i, ada):
                        for j in range(2):
                            load_raw(i * 2 + (DOWN_BASE + j), j, down_src[:, 11 * j:11 * j + 11, bass.ds(i * P, P)],
                                     11 * P)
                            if ada:
                                load_ada(i * 2 + (DOWN_BASE + j + ADA_FIRST), j, 1, (i * 2 + (34 + j)) * P)
                    with sp.Fori(0, 7) as i:
                        down(i, True)
                    down(7, False)

            wg, wu, wd = (a[k][0] for k in ("w_exp_gate", "w_exp_up", "w_exp_down"))

            def load_job(job, e, first=False):
                g = wg[bass.ds(e, 1)].rearrange("e (k p) n -> p (e k) n", p=P)
                u = wu[bass.ds(e, 1)].rearrange("e (k p) n -> p (e k) n", p=P)
                d = wd[bass.ds(e, 1)].rearrange("e (k p) n -> p (e k) n", p=P)
                for n in range(JCH):
                    if not (first and n < 3):
                        sp.wait_ge(m_lo, job * JCH + (n - 2))
                    if n < 22:
                        src = (g, u)[n % 2][:, :, (n // 2) * CW:(n // 2 + 1) * CW]
                    else:
                        src = d[:, 2 * (n - 22):2 * (n - 22) + 2, :]
                    sp.dma_start(MRAW[:, n % 3, :].rearrange("p (k n) -> p k n", k=src.shape[1]),
                                 src).then_inc(m_raw[n % 3], 16)

            sp.wait_ge(chunk_used, CHUNKS)
            sp.wait_ge(psum_out, CHUNKS)
            load_job(0, 0, first=True)
            with sp.Fori(1, NE) as job:
                load_job(job, job)
            sp.wait_ge(sem("routed"), 1)
            extra = sp.value_load(XI[0:1, 4:5], min_val=0, max_val=EXTRA)
            with sp.Fori(0, EXTRA) as k:
                with sp.If(k < extra):
                    e = sp.value_load(XI[0:1, bass.ds(k, 1)], min_val=0, max_val=NE - 1)
                    load_job(k + NE, e)

        @block.vector
        def _(dve):
            see = Seen(dve)
            V = nc.vector

            def lo(c, r, j):
                if isinstance(c, int) and c >= CHUNKS:
                    return
                dve.wait_ge(hi_made, c + 1)
                V.tensor_tensor(WLO[:, j, :], RAW[:, j, :], WHI[:, j, :].bitcast(F32),
                                ALU.subtract).then_inc(lo_made, 1)

            def ada_out(t):
                dve.wait_ge(ada_used, t + 1)
                V.tensor_scalar(MOD[:, bass.ds(t, 1), :], PS[:, 7:8, 0:SEQS], VEC[:, 0, bass.ds(t, 1)], None,
                                ALU.add).then_inc(ada_made, 1)

            def after(l, c, r, j):
                lo(c + 2, r + 1, j)
                if l == 0:
                    ada_out(c + ADA_FIRST)

            x = [0]

            def aux():
                see.next(aux_in)
                x[0] += 1
                return 4 + (x[0] - 1) % 2

            def st(ins):
                see.step(ins, dve_step)

            def v3(t):
                return t[:, 0:KD * T].rearrange("p (k t) -> p k t", k=KD)

            def stats_dve(n, size):
                see.next(stat_in)
                V.tensor_scalar(RST[:, 0:n], PS[:, 6, 0:n], 1.0 / size, EPS, ALU.mult, ALU.add).then_inc(ms_made, 1)
                see.next(std_made)
                st(V.reciprocal(RSTD[:, 0:n], RST[:, 0:n]))

            def rb():
                return RSTD[:, 0:T].unsqueeze(1).broadcast_to([P, KD, T])

            def seq(m):
                return m[:, :, 1:SEQS].unsqueeze(3).broadcast_to([P, KD, NS, LS])

            def samples(t):
                return t[:, :, TP:T].rearrange("p k (s t) -> p k s t", s=NS)

            def pre_norm_dve(l, w, sh, sc, hi_t, lo_t):
                dve.wait_ge(ada_made, sc + KD)
                st(V.scalar_tensor_tensor(AM[:, :, :], MOD[:, sc:sc + KD, :], 1.0,
                                          VEC[:, 1, w + 8 * l:w + 8 * l + 8].unsqueeze(2).broadcast_to([P, KD, SEQS]),
                                          ALU.add, ALU.mult))
                stats_dve(T, D)
                see.step(V.tensor_tensor(HT[:, :, :], X[:, :, :], rb(), ALU.mult), sem("xr_made"))
                st(V.tensor_tensor(samples(HT), samples(HT), seq(AM), ALU.mult))
                see.step(V.tensor_tensor(samples(HT), samples(HT), seq(MOD[:, sh:sh + KD, :]), ALU.add),
                         sem("hs_made"))
                if hi_t is None:
                    return
                see.next(sem("h_hi"))
                V.tensor_tensor(v3(lo_t), HT[:, :, :], v3(hi_t).bitcast(F32), ALU.subtract).then_inc(operand, 1)

            def post_norm_dve(l, w, g, last=False):
                st(V.tensor_tensor(AM[:, :, :], MOD[:, g:g + KD, :],
                                   VEC[:, 1, w + 8 * l:w + 8 * l + 8].unsqueeze(2).broadcast_to([P, KD, SEQS]),
                                   ALU.mult))
                stats_dve(T, D)
                st(V.tensor_tensor(SA[:, :, :], SA[:, :, :], rb(), ALU.mult))
                for d in range(KD):
                    V.scalar_tensor_tensor(X[:, d, 0:TP], SA[:, d, 0:TP], AM[:, d, 0:1], X[:, d, 0:TP],
                                           ALU.mult, ALU.add)
                st(V.tensor_tensor(samples(SA), samples(SA), seq(AM), ALU.mult))
                see.step(V.tensor_tensor(X[:, :, TP:T], X[:, :, TP:T], SA[:, :, TP:T], ALU.add), x_ready)

            for k in range(5):
                b = aux()
                if k < 4:
                    t, h = k // 2, k % 2
                    V.tensor_copy(X[:, 4 * h:4 * h + 4, t * P:(t + 1) * P],
                                  PS[:, b, :].rearrange("p (k t) -> p k t", k=4)).then_inc(aux_out, 1)
                else:
                    V.tensor_copy(X[:, :, TP:T], PS[:, b, :].rearrange("p (k t) -> p k t", k=KD)).then_inc(aux_out, 1)
            dve.wait_ge(aux_out, 5)
            b = aux()
            V.tensor_copy(VEC[:, 0, 0:96], PS[:, b, 0:96])
            V.tensor_copy(VEC[:, 1, 0:82], PS[:, b, P:P + 82]).then_inc(aux_out, 1)
            b = aux()
            V.tensor_copy(CS[:, :, :], PS[:, b, 0:P].rearrange("p (k t) -> p k t", k=KD)[:, :, 0:SEQS])\
                .then_inc(aux_out, 1)
            dve.wait_ge(aux_out, 7)
            lb0, lb1 = VEC[:, 1, 64:72], VEC[:, 1, 72:80]
            st(V.tensor_tensor(LT[:, 2, :], lb0, lb1, ALU.max))
            V.tensor_tensor(LT[:, 0:2, :], VEC[:, 1, 64:80].rearrange("p (l k) -> p l k", l=2),
                            LT[:, 2:3, :].broadcast_to([P, 2, KD]), ALU.subtract).then_inc(sem("lb_shifted"), 1)
            see.next(sem("lb_exp"))
            st(V.tensor_tensor(LT[:, 2, :], LT[:, 0, :], LT[:, 1, :], ALU.add))
            st(V.reciprocal(LT[:, 2, :], LT[:, 2, :]))
            st(V.tensor_tensor(LT[:, 0:2, :], LT[:, 0:2, :], LT[:, 2:3, :].broadcast_to([P, 2, KD]), ALU.mult))
            st(V.tensor_tensor(LT[:, 1, :], LT[:, 0, :], LT[:, 1, :], ALU.add))
            st(V.tensor_tensor(LB[:, :, :], LT[:, 0:2, :], LT[:, 0:1, :].broadcast_to([P, 2, KD]), ALU.subtract))
            st(V.tensor_scalar(OML[:, :, :], LB[:, :, :], -1.0, 1.0, ALU.mult, ALU.add))
            for t in range(ADA_FIRST):
                ada_out(t)
            lo(0, 0, 0)
            lo(1, 0, 1)

            for l in range(DEPTH):
                def only(c, r, j, n):
                    after(l, c, r, j)

                pre_norm_dve(l, 0, ADA_TILES * l, ADA_TILES * l + 8, H1H, H1L)
                through(dve, BASE[l, "f"], 4, only)
                dve.wait_ge(psum_out, BASE[l, "f"] + 4)
                for h in range(HEADS):
                    V.tensor_scalar(FG[:, h, :], FG[:, h, :], OML[:, l, h:h + 1], LB[:, l, h:h + 1], ALU.mult, ALU.add)
                    ins = V.tensor_scalar(KK[:, h, :], KK[:, h, :], OML[:, l, h:h + 1], None, ALU.mult)
                ins.then_inc(sem("k_ready"), 1)
                see.next(sem("k_ready"))
                through(dve, BASE[l, "q"], 4, only)
                through(dve, BASE[l, "i"], 4, only)

                def scores(level, units):
                    for k in range(units):
                        b = aux()
                        if k < 4:
                            src = PS[:, b, :].rearrange("p (h t) -> p h t", h=4)
                            dst = SC[:, k * 512:(k + 1) * 512].rearrange("p (h t) -> p h t", h=4)
                            m = CM[:, level:level + 1, :].broadcast_to([P, 4, P])
                        else:
                            src = PS[0:TS, b, :].rearrange("p (h t) -> p h t", h=8)
                            dst = SC[0:TS, 2048:2560].rearrange("p (h t) -> p h t", h=8)
                            m = CM[0:TS, level:level + 1, 0:TS].broadcast_to([TS, 8, TS])
                        V.copy_predicated(dst, m, src).then_inc(aux_out, 1)
                        dve.wait_ge(aux_out, x[0])

                def level(n):
                    m = LEVELS[n]
                    units = 5 if m < LS else 4
                    scores(n + 1, units)
                    toks = T if m < LS else TP
                    nb = toks // (2 * m)
                    bufs = [FG, BA, BB]
                    cur = FG if n == 0 else (BA, BB)[(n - 1) % 2]
                    nxt = (BA, BB)[n % 2]
                    if n == 0:
                        c4 = FG[:, :, :].rearrange("p h (b two) -> p h b two", two=2)
                    else:
                        c4 = cur[:, 0:HEADS * (toks // m)].rearrange("p (h b two) -> p h b two", h=HEADS, two=2)
                    q5 = QQ[:, :, 0:toks].rearrange("p h (b two m) -> p h b two m", two=2, m=m)
                    k5 = KK[:, :, 0:toks].rearrange("p h (b two m) -> p h b two m", two=2, m=m)
                    shape = [P, HEADS, nb, m]

                    def each(t5, half, b4):
                        bc = b4.unsqueeze(3).broadcast_to(shape)
                        return V.tensor_tensor(t5[:, :, :, half, :], t5[:, :, :, half, :], bc, ALU.mult)
                    each(q5, 1, c4[:, :, :, 0])
                    st(each(k5, 0, c4[:, :, :, 1]))
                    if m == LS // 2:
                        p4 = cur[:, 0:HEADS * (T // m)].rearrange("p (h b two) -> p h b two", h=HEADS, two=2)
                        V.tensor_tensor(BS[:, :, :], p4[:, :, TP // LS:, 0], p4[:, :, TP // LS:, 1], ALU.mult)
                        p4 = p4[:, :, 0:TP // LS, :]
                        nbo = TP // LS
                    else:
                        p4, nbo = c4, nb
                    if m == LEVELS[-1]:
                        ins = V.tensor_tensor(BP[:, :, :], p4[:, :, :, 0], p4[:, :, :, 1], ALU.mult)
                    else:
                        ins = V.tensor_tensor(nxt[:, 0:HEADS * nbo].rearrange("p (h b) -> p h b", h=HEADS),
                                              p4[:, :, :, 0], p4[:, :, :, 1], ALU.mult)
                    ins.then_inc(sem("level_made"), 1)
                    see.next(sem("level_made"))

                dve.wait_ge(psum_out, BASE[l, "i"] + 4)
                see.next(sem("sc_zero"))
                if l == 0:
                    dve.wait_ge(sem("mask_made"), 1)
                for k in range(4):
                    c = BASE[l, "v"] + k
                    after(l, c, c // 2, k % 2)
                    if k == 0:
                        scores(0, 5)
                        see.step(V.tensor_tensor(QQ[:, :, :], QQ[:, :, :], FG[:, :, :], ALU.mult), sem("level_made"))
                    else:
                        level(k - 1)
                dve.wait_ge(psum_out, BASE[l, "v"] + 4)
                for t in range(TT):
                    n = P if t < 2 else TS
                    for h in range(2):
                        ins = V.bn_stats(BN[0:n, t, 6 * h:6 * h + 6], VT[0:n, t, 512 * h:512 * h + 512])
                st(ins)
                for t in range(TT):
                    n = P if t < 2 else TS
                    ins = V.bn_aggr(MV[0:n, t, 0:2], BN[0:n, t, :])
                st(ins)
                if l == 0:
                    st(V.memset(MV[TS:P, 2, :], 1.0))
                V.tensor_scalar(MV[:, :, 2:3], MV[:, :, 1:2], EPS, None, ALU.add).then_inc(sem("var_made"), 1)
                see.next(sem("vstd_made"))
                st(V.reciprocal(MV[:, :, 3:4], MV[:, :, 2:3]))
                dve.wait_ge(sem("ln_in"), 32 * (l + 1))
                for t in range(TT):
                    n = P if t < 2 else TS
                    ins = V.tensor_scalar(VT[0:n, t, :], VT[0:n, t, :], MV[0:n, t, 0:1], MV[0:n, t, 3:4],
                                          ALU.subtract, ALU.mult)
                st(ins)
                for t in range(TT):
                    n = P if t < 2 else TS
                    ins = V.tensor_tensor(VT[0:n, t, :], VT[0:n, t, :], LNW[0:n, :], ALU.mult)
                st(ins)
                for t in range(TT):
                    n = P if t < 2 else TS
                    ins = V.tensor_tensor(VT[0:n, t, :], VT[0:n, t, :], LNB[0:n, :], ALU.add)
                ins.then_inc(sem("v_ready"), 1)
                see.next(sem("v_ready"))
                b = aux()
                V.tensor_tensor(WST[:, :, :], PS[:, b, :].rearrange("p (g t) -> p g t", g=G4),
                                CF[:, C_UPPER:C_UPPER + P].unsqueeze(1).broadcast_to([P, G4, P]), ALU.mult)\
                    .then_inc(aux_out, 1)
                b = aux()
                V.tensor_tensor(WSS[:, :, :], PS[0:TS, b, 0:G4 * TS].rearrange("p (g t) -> p g t", g=G4),
                                CF[0:TS, C_UPPER:C_UPPER + TS].unsqueeze(1).broadcast_to([TS, G4, TS]), ALU.mult)\
                    .then_inc(aux_out, 1)
                for k in range(4):
                    c = BASE[l, "u"] + k
                    lo(c + 2, (c + 2) // 2, k % 2)
                    if l == 0:
                        ada_out(c + ADA_FIRST)
                    dve.wait_ge(psum_out, c + 1)
                    if k:
                        see.next(sem("a_lo"))
                    see.next(sem("mixed"))
                    see.step(V.tensor_tensor(T2[:, :, :], T1[:, 0], PS[:, 4:6, 0:T], ALU.mult), sem("a_made"))
                    see.next(sem("a_hi"))
                    V.tensor_tensor(v3(H2L)[:, 2 * k:2 * k + 2, :], T2[:, :, :],
                                    v3(H2H)[:, 2 * k:2 * k + 2, :].bitcast(F32), ALU.subtract).then_inc(sem("a_lo"), 1)
                    if k in (1, 3):
                        level(3 + k // 2)
                see.next(sem("a_lo"))
                for k in range(4):
                    c = BASE[l, "g"] + k
                    after(l, c, c // 2, k % 2)
                    if k in (1, 3):
                        level(5 + k // 2)
                for k in range(4):
                    c = BASE[l, "A"] + k
                    after(l, c, c // 2, k % 2)
                    if k == 0:
                        for n in range(4):
                            b = aux()
                            V.tensor_copy(KTM[:, n // 2, 512 * (n % 2):512 * (n % 2) + 512],
                                          PS[:, b, :]).then_inc(aux_out, 1)
                        for n in range(2):
                            b = aux()
                            V.tensor_copy(KTM[0:TS, 2, 512 * n:512 * n + 512], PS[0:TS, b, :]).then_inc(aux_out, 1)
                    if k == 1:
                        for n in range(2):
                            b = aux()
                            V.tensor_copy(ST[:, 0, 4 * n:4 * n + 4, :],
                                          PS[:, b, :].rearrange("p (h v) -> p h v", h=4)).then_inc(aux_out, 1)
                        dve.wait_ge(aux_out, x[0])
                    if k == 2:
                        for n in range(2):
                            b = aux()
                            for h in range(4):
                                ins = V.scalar_tensor_tensor(ST[:, 1, 4 * n + h, :], ST[:, 0, 4 * n + h, :],
                                                             BP[:, 4 * n + h, 1:2], PS[:, b, h * P:(h + 1) * P],
                                                             ALU.mult, ALU.add)
                            ins.then_inc(aux_out, 1)
                        dve.wait_ge(aux_out, x[0])
                        mark["s2", l] = x[0]

                def o_norm(dst, g):
                    stats_dve(512, P)
                    st(V.tensor_tensor(ON[:, :], OT[:, :], RSTD[:, :], ALU.mult))
                    v = ON[:, :].rearrange("p (h t) -> p h t", h=dst.shape[1])
                    see.step(V.scalar_tensor_tensor(dst, v, VEC[:, 1, 80 + l:81 + l], g, ALU.mult, ALU.mult),
                             sem("on_made"))

                for k in range(4):
                    c = BASE[l, "ga"] + k
                    after(l, c, c // 2, k % 2)
                    dve.wait_ge(psum_out, c + 1)
                    see.step(V.tensor_tensor(SA[:, 2 * k:2 * k + 2, :], SA[:, 2 * k:2 * k + 2, :], T1[:, 1],
                                             ALU.mult), sem("ga_used"))
                    b = aux()
                    V.tensor_copy(OT[:, :], PS[:, b, :]).then_inc(aux_out, 1)
                    dve.wait_ge(aux_out, x[0])
                    mark["o", l, k] = x[0]
                    o_norm(HT[:, 2 * k:2 * k + 2, 0:TP], GS[:, 2 * k:2 * k + 2, 0:TP])
                for k in range(4):
                    c = BASE[l, "gb"] + k
                    after(l, c, c // 2, k % 2)
                    for s in (2 * k, 2 * k + 1):
                        dve.wait_ge(sem("st_decayed"), 8 * l + s + 1)
                        for n in range(2):
                            b = aux()
                            ins = V.tensor_tensor(ST[:, s % 2, 4 * n:4 * n + 4, :], ST[:, s % 2, 4 * n:4 * n + 4, :],
                                                  PS[:, b, :].rearrange("p (h v) -> p h v", h=4), ALU.add)
                            ins.then_inc(aux_out, 1)
                        mark["st", l, s] = x[0]
                dve.wait_ge(sem("st_read"), 8 * l + 8)
                see.step(V.tensor_copy(OT[:, :], PS[:, 6, :]), sem("os_out"))
                o_norm(HT[:, :, TP:T], GS[:, :, TP:T])
                see.next(sem("h_hi"))
                V.tensor_tensor(v3(H1L), HT[:, :, :], v3(H1H).bitcast(F32), ALU.subtract).then_inc(operand, 1)
                for k in range(4):
                    c = BASE[l, "B"] + k
                    after(l, c, c // 2, k % 2)
                    dve.wait_ge(psum_out, c + 1)
                    st(V.tensor_tensor(T2[:, :, :], T1[:, 0], GB[:, 2 * k:2 * k + 2, :], ALU.mult))
                    see.step(V.tensor_tensor(SA[:, 2 * k:2 * k + 2, :], SA[:, 2 * k:2 * k + 2, :], T2[:, :, :],
                                             ALU.add), sem("merged"))
                    see.next(sem("merged_hi"))
                    V.tensor_tensor(v3(H2L)[:, 2 * k:2 * k + 2, :], SA[:, 2 * k:2 * k + 2, :],
                                    v3(H2H)[:, 2 * k:2 * k + 2, :].bitcast(F32), ALU.subtract)\
                        .then_inc(sem("merged_lo"), 1)
                through(dve, BASE[l, "O"], 4, only, loop=(l == 0))
                post_norm_dve(l, 16, ADA_TILES * l + 16)
                pre_norm_dve(l, 32, ADA_TILES * l + 24, ADA_TILES * l + 32, *((H1H, H1L) if l == 0 else (None, None)))
                if l == 0:
                    states_stored(dve, 0)
                    with dve.Fori(0, 11) as i:
                        for j in range(2):
                            c = i * 2 + (GU_BASE + j)
                            lo(c + 2, None, j)
                            ada_out(c + ADA_FIRST)
                        dve.wait_ge(psum_out, i * 2 + (GU_BASE + 2))
                        dve.wait_ge(sem("ffn_lo"), i)
                        V.tensor_tensor(T2[:, :, :], T1[:, 0], T1[:, 1], ALU.mult).then_inc(sem("ffn_prod"), 1)
                        dve.wait_ge(sem("ffn_hi"), i + 1)
                        V.tensor_tensor(PRL[:, bass.ds(i * 2, 2), :], T2[:, :, :],
                                        PRH[:, bass.ds(i * 2, 2), :].bitcast(F32), ALU.subtract)\
                            .then_inc(sem("ffn_lo"), 1)
                    with dve.Fori(0, 7) as i:
                        for j in range(2):
                            c = i * 2 + (DOWN_BASE + j)
                            lo(c + 2, None, j)
                            ada_out(c + ADA_FIRST)
                    for j in range(2):
                        lo(CHUNKS - 44 + j, None, j)
                    post_norm_dve(l, 48, ADA_TILES * l + 40)

            dve.wait_ge(sem("wr_in"), 32)
            st(V.memset(LG[:, :, :], 0.0))
            b = aux()
            V.tensor_tensor(LG[:, 0:2, :], PS[:, b, 0:16].rearrange("p (t e) -> p t e", e=8),
                            BR[:, :].unsqueeze(1).broadcast_to([P, 2, NE]), ALU.add)
            V.tensor_tensor(LG[0:TS, 2, :], PS[0:TS, b, 16:24], BR[0:TS, :], ALU.add).then_inc(aux_out, 1)
            dve.wait_ge(aux_out, x[0])
            for t in range(TT):
                ins = V.max(TOPV[:, t, :], LG[:, t, :])
            st(ins)
            for t in range(TT):
                ins = V.max_index(TOPI[:, t, :], TOPV[:, t, :], LG[:, t, :])
            st(ins)
            st(V.tensor_copy(TOPF[:, :, :], TOPI[:, :, 0:2]))
            V.tensor_tensor(PR[:, :, 0:1], TOPV[:, :, 1:2], TOPV[:, :, 0:1], ALU.subtract).then_inc(sem("top_made"), 1)
            io = CF[:, C_IOTA8:C_IOTA8 + 8].unsqueeze(1).broadcast_to([P, TT, NE])
            V.tensor_tensor(S1[:, :, :], io, TOPF[:, :, 0:1].broadcast_to([P, TT, NE]), ALU.is_equal)
            st(V.tensor_tensor(S2[:, :, :], io, TOPF[:, :, 1:2].broadcast_to([P, TT, NE]), ALU.is_equal))
            st(V.tensor_tensor(SEL[:, :, :], S1[:, :, :], S2[:, :, :], ALU.add))
            see.step(V.memset(SEL[TS:P, 2, :], 0.0), sem("sel_made"))
            see.next(sem("top_exp"))
            st(V.tensor_scalar(PR[:, :, 1:2], PR[:, :, 0:1], 1.0, None, ALU.add))
            st(V.reciprocal(PR[:, :, 2:3], PR[:, :, 1:2]))
            st(V.tensor_tensor(PR[:, :, 3:4], PR[:, :, 0:1], PR[:, :, 2:3], ALU.mult))
            V.tensor_tensor(S1[:, :, :], S1[:, :, :], PR[:, :, 2:3].broadcast_to([P, TT, NE]), ALU.mult)
            st(V.tensor_tensor(S2[:, :, :], S2[:, :, :], PR[:, :, 3:4].broadcast_to([P, TT, NE]), ALU.mult))
            st(V.tensor_tensor(WT[:, :, :], S1[:, :, :], S2[:, :, :], ALU.add))
            b = aux()
            posv = PS[:, b, 0:32].rearrange("p (t e) -> p t e", e=8)
            V.tensor_copy(POS[:, :, :], posv[:, 0:TT, :])
            V.tensor_copy(CNT[:, 0, :], posv[:, 3, :]).then_inc(aux_out, 1)
            dve.wait_ge(aux_out, x[0])
            st(V.tensor_scalar(POS[:, :, :], POS[:, :, :], 1e6, None, ALU.add))
            st(V.tensor_tensor(POS[:, :, :], POS[:, :, :], SEL[:, :, :], ALU.mult))
            st(V.tensor_scalar(POS[:, :, :], POS[:, :, :], -1e6, None, ALU.add))
            V.tensor_copy(POSJ[:, :, 0:NE], POS[:, :, :])
            V.tensor_copy(WJ[:, :, 0:NE], WT[:, :, :])
            V.memset(POSJ[:, :, JOBS:], -1.0)
            V.memset(WJ[:, :, JOBS:], 0.0)
            V.tensor_scalar(CNT[:, 1, :], CNT[:, 0, :], float(P), None, ALU.is_gt)
            st(V.tensor_scalar(CNT[:, 2, :], CNT[:, 0, :], float(2 * P), None, ALU.is_gt))
            st(V.tensor_tensor(CNT[:, 3, :], CNT[:, 1, :], CNT[:, 2, :], ALU.add))
            st(V.memset(CNT[:, 4, 0:1], 0.0))
            for e in range(1, NE):
                st(V.tensor_tensor(CNT[:, 4, e:e + 1], CNT[:, 4, e - 1:e], CNT[:, 3, e - 1:e], ALU.add))
            st(V.tensor_tensor(CNT[:, 5, :], CNT[:, 4, :], CNT[:, 3, :], ALU.add))
            for k in range(EXTRA):
                V.tensor_scalar(OH[:, 0, :], CNT[:, 4, :], float(k), None, ALU.is_le)
                st(V.tensor_scalar(OH[:, 1, :], CNT[:, 5, :], float(k), None, ALU.is_gt))
                st(V.tensor_tensor(OH[:, 0, :], OH[:, 0, :], OH[:, 1, :], ALU.mult))
                st(V.tensor_scalar(OH[:, 1, :], CNT[:, 4, :], float(P), -float(P * (1 + k)), ALU.mult, ALU.add))
                st(V.tensor_tensor(JT[:, :, :], POS[:, :, :], OH[:, 1:2, :].broadcast_to([P, TT, NE]), ALU.add))
                st(V.tensor_scalar(JT[:, :, :], JT[:, :, :], 1.0, None, ALU.add))
                st(V.tensor_tensor(JT[:, :, :], JT[:, :, :], OH[:, 0:1, :].broadcast_to([P, TT, NE]), ALU.mult))
                st(V.tensor_reduce(POSJ[:, :, NE + k], JT[:, :, :], AX.X, ALU.add))
                st(V.tensor_scalar(POSJ[:, :, NE + k], POSJ[:, :, NE + k], -1.0, None, ALU.add))
                st(V.tensor_tensor(JT[:, :, :], WT[:, :, :], OH[:, 0:1, :].broadcast_to([P, TT, NE]), ALU.mult))
                st(V.tensor_reduce(WJ[:, :, NE + k], JT[:, :, :], AX.X, ALU.add))
                st(V.tensor_tensor(OH[:, 2, :], OH[:, 0, :], CF[:, C_IOTA8:C_IOTA8 + 8], ALU.mult))
                st(V.tensor_reduce(XF[:, k:k + 1], OH[:, 2, :], AX.X, ALU.add))
            st(V.tensor_copy(XF[:, 4:5], CNT[:, 5, NE - 1:NE]))
            V.tensor_copy(XI[0:1, 0:5], XF[0:1, 0:5]).then_inc(sem("routed"), 1)
            see.next(sem("routed"))
            mark["hm"] = x[0]
            for k in range(6):
                b = aux()
                dst, src = hm_unit(HML, k, x[0] - 1)
                see.next(sem("hm_hi"))
                V.tensor_tensor(dst, src, hm_unit(HMH, k, 0)[0].bitcast(F32), ALU.subtract).then_inc(aux_out, 1)
                dve.wait_ge(aux_out, x[0])
            st(V.memset(SA[:, :, :], 0.0))

            def choose(job):
                for t in range(TT):
                    V.tensor_scalar(PM[:, t, :], CF[:, C_IOTA:C_IOTA + P], POSJ[:, t, bass.ds(job, 1)], None,
                                    ALU.is_equal)
                    ins = V.tensor_scalar(PW[:, t, :], CF[:, C_IOTA:C_IOTA + P], POSJ[:, t, bass.ds(job, 1)],
                                          WJ[:, t, bass.ds(job, 1)], ALU.is_equal, ALU.mult)
                ins.then_inc(p_made, 1)

            choose(0)

            states_stored(dve, 1)

            def job_dve(job):
                def m_lo_part(n):
                    dve.wait_ge(m_hi, job * JCH + (n + 1))
                    V.tensor_tensor(MLO[:, n % 3, :], MRAW[:, n % 3, :], MHI[:, n % 3, :].bitcast(F32),
                                    ALU.subtract).then_inc(m_lo, 1)

                m_lo_part(0)
                for k in range(4):
                    dve.wait_ge(m_aux_in, job * JAUX + (k + 1))
                    V.tensor_copy((XEH, XEL)[k // 2][:, 4 * (k % 2):4 * (k % 2) + 4, :],
                                  PS[:, 4 + k % 2, :].rearrange("p (k n) -> p k n", k=4)).then_inc(m_aux_out, 1)
                m_lo_part(1)
                m_lo_part(2)

                def gt_low(p):
                    dve.wait_ge(gt_hi, job * 11 + (p + 1))
                    V.tensor_tensor(GTL[:, 2 * p:2 * p + 2, :],
                                    PS[:, 4 + p % 2, 0:2 * P].rearrange("p (k n) -> p k n", k=2),
                                    GTH[:, 2 * p:2 * p + 2, :].bitcast(F32), ALU.subtract).then_inc(m_aux_out, 1)

                for n in range(JCH):
                    if n < 22 and n % 2:
                        dve.wait_ge(gate_out, job * 11 + (n // 2 + 1))
                        dve.wait_ge(m_used, job * JCH + (n + 1))
                        g = SG[:, (n // 2) * CW:(n // 2 + 1) * CW]
                        V.tensor_tensor(g, g, PS[:, n % 4, 0:CW], ALU.mult).then_inc(prod_made, 1)
                    if n + 3 < JCH:
                        m_lo_part(n + 3)
                    if n < 22 and n % 2 and n > 1:
                        gt_low(n // 2 - 1)
                    if n == 21:
                        gt_low(10)
                        dve.wait_ge(m_aux_in, job * JAUX + 16)
                        V.tensor_copy(PTS[:, :], PS[:, 5, 0:T]).then_inc(m_aux_out, 1)
                        choose(job + 1)
                for d in range(KD):
                    dve.wait_ge(m_aux_in, job * JAUX + (17 + d))
                    V.tensor_tensor(SA[:, d, :], SA[:, d, :], PS[:, 4 + d % 2, 0:T], ALU.add).then_inc(m_aux_out, 1)

            with dve.Fori(0, NE) as job:
                dve.wait_ge(m_aux_out, job * JAUX)
                dve.wait_ge(p_made, job + 1)
                job_dve(job)
            dve.wait_ge(sem("routed"), 1)
            extra = dve.value_load(XI[0:1, 4:5], min_val=0, max_val=EXTRA)
            with dve.Fori(0, EXTRA) as k:
                with dve.If(k < extra):
                    dve.wait_ge(m_aux_out, (k + NE) * JAUX)
                    dve.wait_ge(p_made, k + (NE + 1))
                    job_dve(k + NE)
            dve.wait_ge(m_aux_out, (extra + NE) * JAUX)
            post_norm_dve(1, 48, ADA_TILES + 40)
            for k in range(6):
                b = aux()
                t, h = k // 2, k % 2
                n = P if t < 2 else TS
                ins = V.tensor_copy(XTM[0:n, t, 512 * h:512 * h + 512], PS[0:n, b, :])
                ins.then_inc(aux_out, 1)
            mark["y"] = x[0]

        @block.scalar
        def _(act):
            see = Seen(act)
            A = nc.scalar

            def hi(c, r, j):
                if isinstance(c, int) and c >= CHUNKS:
                    return
                act.wait_ge(raw_in[j], r * 16 + 16)
                if not (isinstance(c, int) and c < 2):
                    act.wait_ge(chunk_used, c - 1)
                A.activation(WHI[:, j, :], RAW[:, j, :], ACT.Copy).then_inc(hi_made, 1)

            def stats_act(src):
                A.activation(SQ[:, :, :], src, ACT.Square).then_inc(sq_made, 1)
                see.next(ms_made)
                A.activation(RST[:, 0:T], RST[:, 0:T], ACT.Sqrt).then_inc(std_made, 1)

            def pre_norm_act(l, sh, parts):
                if l or sh:
                    see.next(x_ready)
                else:
                    act.wait_ge(aux_out, 5)
                stats_act(X[:, :, :])
                see.next(sem("xr_made"))
                for d in range(KD):
                    ins = A.activation(HT[:, d, 0:TP], HT[:, d, 0:TP], ACT.Identity,
                                       bias=MOD[:, sh + d, 0:1], scale=AM[:, d, 0:1])
                ins.then_inc(sem("hp_made"), 1)
                if parts is None:
                    return
                see.next(sem("hp_made"))
                act.wait_ge(sem("hs_made"), see.n[id(sem("hp_made"))])
                A.activation(parts[:, 0:KD * T].rearrange("p (k t) -> p k t", k=KD), HT[:, :, :],
                             ACT.Copy).then_inc(sem("h_hi"), 1)

            def v3(t):
                return t[:, 0:KD * T].rearrange("p (k t) -> p k t", k=KD)

            act.wait_ge(sem("c_in"), 32)
            A.activation(CT[:, :], CT[:, :], ACT.Silu).then_inc(sem("c_made"), 1)
            see.next(sem("lb_shifted"))
            A.activation(LT[:, 0:2, :], LT[:, 0:2, :], ACT.Exp).then_inc(sem("lb_exp"), 1)
            hi(0, 0, 0)
            hi(1, 0, 1)
            for l in range(DEPTH):
                pre_norm_act(l, ADA_TILES * l, H1H)

                def banks(j):
                    return PS[:, 2 * j:2 * j + 2, 0:T]

                def plain(dst, func, scale=1.0):
                    def one(c, r, j, n):
                        act.wait_ge(chunk_used, c + 1)
                        A.activation(dst[:, bass.ds(n * 2, 2), :], banks(j), func, scale=scale).then_inc(psum_out, 1)
                        hi(c + 2, r + 1, j)
                    return one

                def gates(c, r, j, n):
                    act.wait_ge(chunk_used, c + 1)
                    A.activation(KK[:, bass.ds(n * 2, 2), :], banks(j), ACT.Sigmoid, scale=-1.0)
                    A.activation(FG[:, bass.ds(n * 2, 2), :], banks(j), ACT.Sigmoid).then_inc(psum_out, 1)
                    hi(c + 2, r + 1, j)

                def token_major(dst, func):
                    def one(c, r, j, n):
                        act.wait_ge(chunk_used, c + 1)
                        A.activation(dst[:, 0:2, bass.ds(n * CW, CW)],
                                     PS[:, 2 * j, :].rearrange("p (t n) -> p t n", t=2), func)
                        A.activation(dst[0:TS, 2, bass.ds(n * CW, CW)], PS[0:TS, 2 * j + 1, 0:CW],
                                     func).then_inc(psum_out, 1)
                        hi(c + 2, r + 1, j)
                    return one

                through(act, BASE[l, "f"], 4, gates)
                through(act, BASE[l, "q"], 4, plain(QQ, ACT.Silu))
                through(act, BASE[l, "i"], 4, token_major(IT, ACT.Copy))
                through(act, BASE[l, "v"], 4, token_major(VT, ACT.Gelu), loop=False)
                see.next(sem("var_made"))
                A.activation(MV[:, :, 2:3], MV[:, :, 2:3], ACT.Sqrt).then_inc(sem("vstd_made"), 1)

                for k in range(4):
                    c, j = BASE[l, "u"] + k, k % 2
                    act.wait_ge(chunk_used, c + 1)
                    if k or l:
                        act.wait_ge(sem("a_made"), 4 * l + k)
                    A.activation(T1[:, 0], banks(j), ACT.Gelu).then_inc(psum_out, 1)
                    hi(c + 2, (c + 2) // 2, j)
                    act.wait_ge(sem("a_made"), 4 * l + k + 1)
                    A.activation(v3(H2H)[:, 2 * k:2 * k + 2, :], T2[:, :, :], ACT.Copy).then_inc(sem("a_hi"), 1)
                act.wait_ge(sem("v_stored"), 16 * (l + 1))
                act.wait_ge(sem("mixed"), 4 * l + 4)
                through(act, BASE[l, "g"], 4, plain(GS, ACT.Silu), loop=False)
                act.wait_ge(sem("level_made"), 8 * l + 8)
                through(act, BASE[l, "A"], 4, plain(SA, ACT.Copy), loop=False)

                def o_norm():
                    A.activation(OSQ[:, :], OT[:, :], ACT.Square).then_inc(sq_made, 1)
                    see.next(ms_made)
                    A.activation(RST[:, :], RST[:, :], ACT.Sqrt).then_inc(std_made, 1)

                for k in range(4):
                    c, j = BASE[l, "ga"] + k, k % 2
                    act.wait_ge(chunk_used, c + 1)
                    act.wait_ge(sem("ga_used"), 4 * l + k)
                    A.activation(T1[:, 1], banks(j), ACT.Sigmoid).then_inc(psum_out, 1)
                    hi(c + 2, (c + 2) // 2, j)
                    act.wait_ge(aux_out, mark["o", l, k])
                    o_norm()
                for k in range(4):
                    c, j = BASE[l, "gb"] + k, k % 2
                    act.wait_ge(chunk_used, c + 1)
                    A.activation(GB[:, 2 * k:2 * k + 2, :], banks(j), ACT.Sigmoid).then_inc(psum_out, 1)
                    hi(c + 2, (c + 2) // 2, j)
                see.next(sem("os_out"))
                o_norm()
                act.wait_ge(sem("on_made"), 5 * l + 5)
                A.activation(v3(H1H), HT[:, :, :], ACT.Copy).then_inc(sem("h_hi"), 1)
                for k in range(4):
                    c, j = BASE[l, "B"] + k, k % 2
                    act.wait_ge(chunk_used, c + 1)
                    act.wait_ge(sem("merged"), 4 * l + k)
                    A.activation(T1[:, 0], banks(j), ACT.Copy).then_inc(psum_out, 1)
                    hi(c + 2, (c + 2) // 2, j)
                    act.wait_ge(sem("merged"), 4 * l + k + 1)
                    A.activation(v3(H2H)[:, 2 * k:2 * k + 2, :], SA[:, 2 * k:2 * k + 2, :],
                                 ACT.Copy).then_inc(sem("merged_hi"), 1)
                through(act, BASE[l, "O"], 4, plain(SA, ACT.Copy), loop=(l == 0))
                act.wait_ge(psum_out, BASE[l, "O"] + 4)
                stats_act(SA[:, :, :])
                pre_norm_act(l, ADA_TILES * l + 24, H1H if l == 0 else None)
                if l == 0:
                    states_stored(act, 0)
                    with act.Fori(0, 11) as i:
                        for j in range(2):
                            c = i * 2 + (GU_BASE + j)
                            act.wait_ge(chunk_used, c + 1)
                            act.wait_ge(sem("ffn_prod"), i)
                            A.activation(T1[:, j], banks(j), (ACT.Silu, ACT.Copy)[j]).then_inc(psum_out, 1)
                            hi(c + 2, i + (GU_BASE // 2 + 1), j)
                        act.wait_ge(sem("ffn_prod"), i + 1)
                        A.activation(PRH[:, bass.ds(i * 2, 2), :], T2[:, :, :], ACT.Copy).then_inc(sem("ffn_hi"), 1)
                    with act.Fori(0, 4) as i:
                        for u in range(2):
                            c = i * 4 + (DOWN_BASE + 2 * u)
                            r = i * 2 + (DOWN_BASE // 2 + u)
                            act.wait_ge(chunk_used, c + 1)
                            hi(c + 2, r + 1, 0)
                            act.wait_ge(chunk_used, c + 2)
                            A.activation(SA[:, bass.ds(i * 2 + u, 1), :], PS[:, 2 * u:2 * u + 1, 0:T],
                                         ACT.Copy).then_inc(psum_out, 2)
                            hi(c + 3, r + 1, 1)
                    act.wait_ge(psum_out, 82)
                    stats_act(SA[:, :, :])

            see.next(sem("top_made"))
            A.activation(PR[:, :, 0:1], PR[:, :, 0:1], ACT.Exp).then_inc(sem("top_exp"), 1)
            for k in range(6):
                act.wait_ge(aux_in, mark["hm"] + k + 1)
                A.activation(*hm_unit(HMH, k, mark["hm"] + k), ACT.Copy).then_inc(sem("hm_hi"), 1)
            states_stored(act, 1)

            def job_act(job):
                def m_hi_part(n):
                    act.wait_ge(m_raw[n % 3], job * (16 * 11) + 16 * (n // 3 + 1))
                    act.wait_ge(m_used, job * JCH + (n - 2 if n >= 3 else 0))
                    A.activation(MHI[:, n % 3, :], MRAW[:, n % 3, :], ACT.Copy).then_inc(m_hi, 1)

                for n in range(3):
                    m_hi_part(n)

                def gt_high(p):
                    act.wait_ge(m_aux_in, job * JAUX + (5 + p))
                    A.activation(GTH[:, 2 * p:2 * p + 2, :],
                                 PS[:, 4 + p % 2, 0:2 * P].rearrange("p (k n) -> p k n", k=2), ACT.Copy)\
                        .then_inc(gt_hi, 1)

                for n in range(JCH):
                    if n < 22 and n % 2 == 0:
                        act.wait_ge(m_used, job * JCH + (n + 1))
                        A.activation(SG[:, (n // 2) * CW:(n // 2 + 1) * CW], PS[:, n % 4, 0:CW],
                                     ACT.Silu).then_inc(gate_out, 1)
                    if n + 3 < JCH:
                        m_hi_part(n + 3)
                    if n < 22 and n % 2 and n > 1:
                        gt_high(n // 2 - 1)
                    if n == 21:
                        gt_high(10)
                act.wait_ge(m_used, job * JCH + JCH)
                A.activation(YE[:, :].rearrange("p (k n) -> p k n", k=2), PS[:, 6:8, :], ACT.Copy).then_inc(y_made, 1)

            with act.Fori(0, NE) as job:
                job_act(job)
            act.wait_ge(sem("routed"), 1)
            extra = act.value_load(XI[0:1, 4:5], min_val=0, max_val=EXTRA)
            with act.Fori(0, EXTRA) as k:
                with act.If(k < extra):
                    job_act(k + NE)
            act.wait_ge(m_aux_out, (extra + NE) * JAUX)
            stats_act(SA[:, :, :])

        @block.gpsimd
        def _(pool):
            see = Seen(pool)
            small = sem("small_in")
            pool.dma_start(CF[:, :], a["const_f"]).then_inc(small, 16)
            pool.dma_start(SC[:, 0:8 * P].rearrange("p (l t) -> p l t", l=8), a["const_m"]).then_inc(sem("mask_in"), 16)
            xtm = sem("xtm_in")
            pool.dma_start(CT[0:1, :], a["c_prompt"]).then_inc(sem("c_in"), 16)
            pool.dma_start(CT[1:SEQS, :], a["c_sample"]).then_inc(sem("c_in"), 16)
            vec = sem("vec_in")
            pool.dma_start(VR[0:96, 0, :], a["b_ada"].rearrange("l (j p) -> (l j) p", p=P)).then_inc(vec, 16)
            for n, k in enumerate(("norm_pre_mix", "norm_post_mix", "norm_pre_ffn", "norm_post_ffn", "hg_lb_raw")):
                pool.dma_start(VR[16 * n:16 * n + 16, 1, :],
                               a[k].rearrange("l (j p) -> (l j) p", p=P)).then_inc(vec, 16)
            pool.dma_start(VR[80:82, 1, :], a["hg_norm_w"]).then_inc(vec, 16)
            pool.dma_start(XTM[:, 0:2, :], a["x_prompt"][0].rearrange("(t p) d -> p t d", p=P)).then_inc(xtm, 16)
            pool.dma_start(XTM[0:TS, 2, :], a["x_sample"].rearrange("s t d -> (s t) d")).then_inc(xtm, 16)
            pool.memset(ONES[:, :], 1.0).then_inc(sem("ones_set"), 1)
            for t in (H1H, H1L):
                pool.memset(t[:, KD * T:KD * T + 64].bitcast(F32), 0.0).then_inc(sem("tail_set"), 1)

            pool.wait_ge(sem("mask_in"), 16)
            pool.tensor_copy(CM[:, :, :], SC[:, 0:8 * P].rearrange("p (l t) -> p l t", l=8)).then_inc(sem("mask_made"), 1)
            see.next(sem("mask_made"))

            for l in range(DEPTH):
                if l:
                    pool.wait_ge(chunk_used, GU_BASE)
                ws_in, bs_in = sem("ws_in"), sem("bs_in")
                pool.memset(WSRS[:, :, :], 0.0).then_inc(sem("wsrs_zero"), 1)
                pool.dma_start(LNW[:, :], a["gm_ln_w"][l:l + 1, :].broadcast_to([P, D])).then_inc(sem("ln_in"), 16)
                pool.dma_start(LNB[:, :], a["gm_ln_b"][l:l + 1, :].broadcast_to([P, D])).then_inc(sem("ln_in"), 16)
                pool.dma_start(WSR[:, :, :], a["gm_ws"][l].rearrange("g t s -> t g s")).then_inc(ws_in, 16)
                see.next(sem("wsrs_zero"))
                for s in range(NS):
                    pool.dma_start(WSRS[s * LS:(s + 1) * LS, :, s * LS:(s + 1) * LS],
                                   a["gm_ws"][l, :, 0:LS, 0:LS].rearrange("g t s -> t g s")).then_inc(ws_in, 16)
                if l:
                    pool.wait_ge(x_ready, 2)
                for g in range(G4):
                    row = a["gm_bs"][l, g:g + 1, :]
                    for t in range(2):
                        pool.dma_start(BGS[32 * g:32 * g + 1, t * P:(t + 1) * P], row).then_inc(bs_in, 16)
                    pool.dma_start(BGS[32 * g:32 * g + 1, TP:T].rearrange("p (s t) -> p s t", s=NS),
                                   row[:, 0:LS].unsqueeze(1).broadcast_to([1, NS, LS])).then_inc(bs_in, 16)
                pool.memset(SC[:, :], 0.0).then_inc(sem("sc_zero"), 1)
                see.next(sem("v_ready"))
                pool.dma_start(out["v"][l].rearrange("s t d -> (s t) d"), VT[0:TS, 2, :]).then_inc(sem("v_stored"), 16)
                pool.wait_ge(aux_out, mark["s2", l])
                pool.dma_start(out["sp"][l, 0].rearrange("h k v -> k h v"), ST[:, 1]).then_inc(sem("sp_stored"), 16)
                for s in range(NS):
                    if s < 2:
                        if s == 0:
                            pool.wait_ge(aux_out, mark["o", l, 3])
                        else:
                            pool.wait_ge(sem("sp_stored"), 16 * (l + 1))
                    else:
                        pool.wait_ge(sem(f"st_stored{s % 2}"), 16 * (4 * l + s // 2))
                    pool.dma_start(ST[:, s % 2], a["state_hgrn"][l, s].rearrange("h k v -> k h v"))\
                        .then_inc(sem(f"st_in{s % 2}"), 16)
                    if s < 2:
                        pool.wait_ge(sem("sc_used"), l + 1)
                    else:
                        pool.wait_ge(aux_out, mark["st", l, s - 2])
                    pool.tensor_scalar(IM[:, s % 2, :], IT[0:TS, 2, :], CF[0:TS, C_SEQ + s:C_SEQ + s + 1], None,
                                       ALU.mult).then_inc(sem("im_made"), 1)
                    pool.wait_ge(sem("st_read"), 8 * l + s + 1)
                    pool.wait_ge(sem(f"st_in{s % 2}"), 16 * (4 * l + s // 2 + 1))
                    pool.tensor_tensor(ST[:, s % 2], ST[:, s % 2],
                                       BS[:, :, s:s + 1].broadcast_to([P, HEADS, P]), ALU.mult)\
                        .then_inc(sem("st_decayed"), 1)
                    pool.wait_ge(aux_out, mark["st", l, s])
                    pool.dma_start(out["ss"][l, s].rearrange("h k v -> k h v"), ST[:, s % 2])\
                        .then_inc(sem(f"st_stored{s % 2}"), 16)
            pool.wait_ge(chunk_used, CHUNKS)
            pool.dma_start(WR[:, :, :], a["w_router"][0].rearrange("(k p) e -> p k e", p=P)).then_inc(sem("wr_in"), 16)
            pool.dma_start(BR[:, :], a["b_router"][0:1, :].broadcast_to([P, NE])).then_inc(sem("wr_in"), 16)
            pool.wait_ge(aux_out, mark["y"])
            pool.dma_start(out["yp"][0].rearrange("(t p) d -> p t d", p=P), XTM[:, 0:2, :]).then_inc(sem("y_stored"), 16)
            pool.dma_start(out["ys"].rearrange("s t d -> (s t) d"), XTM[0:TS, 2, :]).then_inc(sem("y_stored"), 16)
            pool.wait_ge(sem("v_stored"), 32)
            pool.wait_ge(sem("sp_stored"), 32)
            pool.wait_ge(sem("st_stored0"), 16 * 8)
            pool.wait_ge(sem("st_stored1"), 16 * 8)
            pool.wait_ge(sem("y_stored"), 32)

        @block.tensor
        def _(pe):
            M = nc.tensor
            x = [0]
            counts = {"stat": 0, "sq": 0}

            def aux():
                if x[0] >= 2:
                    pe.wait_ge(aux_out, x[0] - 1)
                x[0] += 1
                return 4 + (x[0] - 1) % 2

            def stats_pe(src, tiles, n):
                counts["sq"] += 1
                pe.wait_ge(sq_made, counts["sq"])
                if counts["sq"] > 1:
                    pe.wait_ge(ms_made, counts["sq"] - 1)
                for k in range(tiles):
                    ins = M.matmul(PS[:, 6, 0:n], ONES[:, :], src(k), start=(k == 0), stop=(k == tiles - 1))
                ins.then_inc(stat_in, 1)

            def ada(t, r, j):
                pe.wait_ge(ada_in[j], r * 16 + 16)
                if not (isinstance(t, int) and t == 0):
                    pe.wait_ge(ada_made, t)
                for k in range(KD):
                    ins = M.matmul(PS[:, 7, 0:SEQS], ADA[:, j, k, :], CS[:, k, :], start=(k == 0), stop=(k == KD - 1))
                ins.then_inc(ada_used, 1)

            def three(out_, w, v, start, stop):
                M.matmul(out_, w[0], v[0], start=start, stop=False)
                M.matmul(out_, w[0], v[1], start=False, stop=False)
                return M.matmul(out_, w[1], v[0], start=False, stop=stop)

            def chunk_start(c):
                pe.wait_ge(lo_made, c + 1)
                if not (isinstance(c, int) and c < 2):
                    pe.wait_ge(psum_out, c - 1)

            def channels(parts, l):
                def one(c, r, j, n):
                    chunk_start(c)
                    for m in range(2):
                        for k in range(KD):
                            s = slice(k * CW + m * P, k * CW + (m + 1) * P)
                            t = slice(k * T, (k + 1) * T)
                            ins = three(PS[:, 2 * j + m, 0:T], (WHI[:, j, s], WLO[:, j, s]),
                                        (parts[0][:, t], parts[1][:, t]), k == 0, k == KD - 1)
                    ins.then_inc(chunk_used, 1)
                    if l == 0:
                        ada(c + ADA_FIRST, r + ADA_FIRST // 2, j)
                return one

            def tokens(parts, l):
                def one(c, r, j, n):
                    chunk_start(c)
                    for t in range(TT):
                        o_ = PS[:, 2 * j + t // 2, CW * (t % 2):CW * (t % 2) + CW]
                        for k in range(KD):
                            s = slice(k * CW, (k + 1) * CW)
                            q = slice(k * T + t * P, k * T + (t + 1) * P)
                            ins = three(o_, (parts[0][:, q], parts[1][:, q]), (WHI[:, j, s], WLO[:, j, s]),
                                        k == 0, k == KD - 1)
                    ins.then_inc(chunk_used, 1)
                    if l == 0:
                        ada(c + ADA_FIRST, r + ADA_FIRST // 2, j)
                return one

            H1, H2 = (H1H, H1L), (H2H, H2L)

            pe.wait_ge(sem("small_in"), 16)
            pe.wait_ge(sem("xtm_in"), 32)
            for k in range(5):
                b = aux()
                if k < 4:
                    for d in range(4):
                        kd = 4 * (k % 2) + d
                        ins = M.transpose(PS[:, b, d * P:(d + 1) * P], XTM[:, k // 2, kd * P:(kd + 1) * P], ident)
                else:
                    for d in range(KD):
                        ins = M.transpose(PS[:, b, d * TS:(d + 1) * TS], XTM[0:TS, 2, d * P:(d + 1) * P],
                                          CF[0:TS, C_ID:C_ID + TS])
                ins.then_inc(aux_in, 1)
            pe.wait_ge(sem("vec_in"), 16 * 7)
            b = aux()
            M.transpose(PS[:, b, 0:96], VR[0:96, 0, :], CF[0:96, C_ID:C_ID + 96])
            M.transpose(PS[:, b, P:P + 82], VR[0:82, 1, :], CF[0:82, C_ID:C_ID + 82]).then_inc(aux_in, 1)
            pe.wait_ge(sem("c_made"), 1)
            b = aux()
            for d in range(KD):
                ins = M.transpose(PS[:, b, d * 16:d * 16 + SEQS], CT[:, d * P:(d + 1) * P], CF[0:SEQS, C_ID:C_ID + SEQS])
            ins.then_inc(aux_in, 1)
            pe.wait_ge(sem("ones_set"), 1)
            pe.wait_ge(aux_out, 7)
            for t in range(ADA_FIRST):
                ada(t, t // 2, t % 2)

            n_operand = 0
            for l in range(DEPTH):
                stats_pe(lambda k: SQ[:, k, :], KD, T)
                n_operand += 1
                pe.wait_ge(operand, n_operand)
                if l == 0:
                    pe.wait_ge(sem("tail_set"), 2)
                through(pe, BASE[l, "f"], 4, channels(H1, l))
                through(pe, BASE[l, "q"], 4, channels(H1, l))
                through(pe, BASE[l, "i"], 4, tokens(H1, l))

                def scores(units):
                    for k in range(units):
                        b = aux()
                        for h in range(4 if k < 4 else 8):
                            if k < 4:
                                hh, t0, n = 4 * (k % 2) + h, P * (k // 2), P
                            else:
                                hh, t0, n = h, TP, TS
                            ins = M.matmul(PS[0:n, b, h * n:(h + 1) * n], KK[:, hh, t0:t0 + n], QQ[:, hh, t0:t0 + n],
                                           start=True, stop=True)
                        ins.then_inc(aux_in, 1)

                def level(n):
                    pe.wait_ge(sem("level_made"), 8 * l + n + 1)
                    scores(5 if LEVELS[n] < LS else 4)

                for k in range(4):
                    c = BASE[l, "v"] + k
                    tokens(H1, l)(c, c // 2, k % 2, k)
                    if k == 0:
                        pe.wait_ge(sem("k_ready"), l + 1)
                        pe.wait_ge(psum_out, BASE[l, "i"] + 4)
                        scores(5)
                    else:
                        level(k - 1)
                pe.wait_ge(sem("ws_in"), 16 * 9 * (l + 1))
                b = aux()
                for g in range(G4):
                    ins = M.transpose(PS[:, b, g * P:(g + 1) * P], WSR[:, g, :], ident)
                ins.then_inc(aux_in, 1)
                b = aux()
                for g in range(G4):
                    ins = M.transpose(PS[0:TS, b, g * TS:(g + 1) * TS], WSRS[:, g, :], CF[0:TS, C_ID:C_ID + TS])
                ins.then_inc(aux_in, 1)
                for k in range(4):
                    c = BASE[l, "u"] + k
                    channels(H1, l)(c, c // 2, k % 2, k)
                    if k == 0:
                        pe.wait_ge(sem("v_ready"), l + 1)
                        pe.wait_ge(sem("bs_in"), 16 * 12 * (l + 1))
                    pe.wait_ge(aux_out, x[0])
                    if k or l:
                        pe.wait_ge(sem("a_made"), 4 * l + k)
                    for m in range(2):
                        n = 2 * k + m
                        g, s = n // 2, slice(n * P, (n + 1) * P)
                        o_ = PS[:, 4 + m, :]
                        M.matmul(o_[:, 0:T], ONES[32 * g:32 * g + 1, :], BGS[32 * g:32 * g + 1, :], start=True, stop=False,
                                 skip_group_check=True)
                        M.matmul(o_[:, 0:P], VT[:, 0, s], WST[:, g, :], start=False, stop=False, skip_group_check=True)
                        M.matmul(o_[:, P:TP], VT[:, 1, s], WST[:, g, :], start=False, stop=False, skip_group_check=True)
                        ins = M.matmul(o_[:, TP:T], VT[0:TS, 2, s], WSS[:, g, :], start=False, stop=True,
                                       skip_group_check=True)
                    ins.then_inc(sem("mixed"), 1)
                    if k in (1, 3):
                        pe.wait_ge(sem("a_made"), 4 * l + k + 1)
                        level(3 + k // 2)
                for k in range(4):
                    c = BASE[l, "g"] + k
                    channels(H1, l)(c, c // 2, k % 2, k)
                    if k in (1, 3):
                        level(5 + k // 2)
                pe.wait_ge(sem("a_lo"), 4 * l + 4)
                for k in range(4):
                    c = BASE[l, "A"] + k
                    channels(H2, l)(c, c // 2, k % 2, k)
                    if k == 0:
                        pe.wait_ge(sem("level_made"), 8 * l + 8)
                        for n in range(4):
                            b = aux()
                            for h in range(4):
                                ins = M.transpose(PS[:, b, h * P:(h + 1) * P],
                                                  KK[:, 4 * (n % 2) + h, P * (n // 2):P * (n // 2) + P], ident)
                            ins.then_inc(aux_in, 1)
                        for n in range(2):
                            b = aux()
                            for h in range(4):
                                ins = M.transpose(PS[0:TS, b, h * P:(h + 1) * P], KK[:, 4 * n + h, TP:T], ident)
                            ins.then_inc(aux_in, 1)
                    if k in (1, 2):
                        pe.wait_ge(aux_out, x[0])
                        for n in range(2):
                            b = aux()
                            for h in range(4):
                                s = slice((4 * n + h) * P, (4 * n + h + 1) * P)
                                ins = M.matmul(PS[:, b, h * P:(h + 1) * P], KTM[:, k - 1, s], IT[:, k - 1, s],
                                               start=True, stop=True)
                            ins.then_inc(aux_in, 1)
                for k in range(4):
                    c = BASE[l, "ga"] + k
                    channels(H1, l)(c, c // 2, k % 2, k)
                    pe.wait_ge(aux_out, x[0])
                    b = aux()
                    for hh in range(2):
                        h = 2 * k + hh
                        s, q = slice(h * P, (h + 1) * P), (h % 4) * P
                        for t in range(2):
                            o_ = PS[:, b, hh * TP + t * P:hh * TP + (t + 1) * P]
                            u0 = (2 * t + h // 4) * 512 + q
                            ins = M.matmul(o_, IT[:, t, s], SC[:, u0:u0 + P], start=True, stop=(t == 0))
                            if t:
                                ins = M.matmul(o_, ST[:, 0, h, :], QQ[:, h, P:TP], start=False, stop=True)
                    ins.then_inc(aux_in, 1)
                    stats_pe(lambda _: OSQ[:, :], 1, 512)
                for k in range(4):
                    c = BASE[l, "gb"] + k
                    channels(H1, l)(c, c // 2, k % 2, k)
                    if k == 0:
                        pe.wait_ge(ms_made, counts["sq"])
                        for h in range(HEADS):
                            ins = M.matmul(PS[:, 6, h * TS:(h + 1) * TS], IT[0:TS, 2, h * P:(h + 1) * P],
                                           SC[0:TS, 2048 + h * TS:2048 + (h + 1) * TS], start=(h == 0), stop=False,
                                           skip_group_check=True)
                        ins.then_inc(sem("sc_used"), 1)
                    for s in (2 * k, 2 * k + 1):
                        pe.wait_ge(sem(f"st_in{s % 2}"), 16 * (4 * l + s // 2 + 1))
                        for h in range(HEADS):
                            t0 = TP + s * LS
                            ins = M.matmul(PS[:, 6, h * TS + s * LS:h * TS + (s + 1) * LS], ST[:, s % 2, h, :],
                                           QQ[:, h, t0:t0 + LS], start=False, stop=(s == NS - 1 and h == HEADS - 1),
                                           skip_group_check=True)
                        ins.then_inc(sem("st_read"), 1)
                        pe.wait_ge(sem("im_made"), 8 * l + s + 1)
                        for n in range(2):
                            b = aux()
                            for h in range(4):
                                q = slice((4 * n + h) * P, (4 * n + h + 1) * P)
                                ins = M.matmul(PS[:, b, h * P:(h + 1) * P], KTM[0:TS, 2, q], IM[:, s % 2, q],
                                               start=True, stop=True)
                            ins.then_inc(aux_in, 1)
                stats_pe(lambda _: OSQ[:, :], 1, 512)
                n_operand += 1
                pe.wait_ge(operand, n_operand)
                through(pe, BASE[l, "B"], 4, channels(H1, l), loop=False)
                pe.wait_ge(sem("merged_lo"), 4 * l + 4)
                through(pe, BASE[l, "O"], 4, channels(H2, l), loop=(l == 0))
                stats_pe(lambda k: SQ[:, k, :], KD, T)
                stats_pe(lambda k: SQ[:, k, :], KD, T)
                if l == 0:
                    n_operand += 1
                    pe.wait_ge(operand, n_operand)
                    with pe.Fori(0, 11) as i:
                        for j in range(2):
                            channels(H1, l)(i * 2 + (GU_BASE + j), i + GU_BASE // 2, j, None)
                    pe.wait_ge(sem("ffn_lo"), 11)

                    def down(u, c, r, with_ada):
                        for j in range(2):
                            pe.wait_ge(lo_made, c + j + 1)
                            if j == 0:
                                pe.wait_ge(psum_out, c - 1 if u is None else c)
                            for k in range(11):
                                s = slice(k * P, (k + 1) * P)
                                kf = 11 * j + k
                                bank = 2 * (0 if u is None else u)
                                ins = three(PS[:, bank, 0:T], (WHI[:, j, s], WLO[:, j, s]),
                                            (PRH[:, kf, :], PRL[:, kf, :]), kf == 0, kf == KF - 1)
                            ins.then_inc(chunk_used, 1)
                            if with_ada:
                                ada(c + j + ADA_FIRST, r + ADA_FIRST // 2, j)
                    with pe.Fori(0, 3) as i:
                        for u in range(2):
                            down(u, i * 4 + (DOWN_BASE + 2 * u), i * 2 + (DOWN_BASE // 2 + u), True)
                    down(0, DOWN_BASE + 12, (DOWN_BASE + 12) // 2, True)
                    down(1, DOWN_BASE + 14, (DOWN_BASE + 14) // 2, False)
                    stats_pe(lambda k: SQ[:, k, :], KD, T)

            pe.wait_ge(sem("hp_made"), 4)
            pe.wait_ge(sem("hs_made"), 4)
            pe.wait_ge(sem("wr_in"), 32)
            b = aux()
            for t in range(TT):
                n = P if t < 2 else TS
                for k in range(KD):
                    ins = M.matmul(PS[0:n, b, 8 * t:8 * t + 8], HT[:, k, t * P:t * P + n], WR[:, k, :],
                                   start=(k == 0), stop=(k == KD - 1))
            ins.then_inc(aux_in, 1)
            pe.wait_ge(sem("sel_made"), 1)
            b = aux()
            for t in range(TT + 1):
                o_ = PS[:, b, 8 * t:8 * t + 8]
                for e in range(min(t, TT)):
                    ins = M.matmul(o_, ONES[:, :], SEL[:, e, :], start=(e == 0), stop=(t == TT and e == TT - 1))
                if t < TT:
                    ins = M.matmul(o_, CF[:, C_TRI:C_TRI + P], SEL[:, t, :], start=(t == 0), stop=True)
            ins.then_inc(aux_in, 1)
            for k in range(6):
                b = aux()
                n, t0 = (P if k < 4 else TS), P * (k // 2)
                for d in range(4):
                    ins = M.transpose(PS[0:n, b, d * P:(d + 1) * P], HT[:, 4 * (k % 2) + d, t0:t0 + n], ident)
                ins.then_inc(aux_in, 1)
            pe.wait_ge(aux_out, x[0])

            def job_pe(job):
                def side(k):
                    pe.wait_ge(m_aux_out, job * JAUX + max(k - 1, 0))
                    return 4 + k % 2

                pe.wait_ge(p_made, job + 1)
                for k in range(4):
                    b = side(k)
                    for d in range(4):
                        s = slice((4 * (k % 2) + d) * P, (4 * (k % 2) + d + 1) * P)
                        for t in range(TT):
                            n = P if t < 2 else TS
                            ins = M.matmul(PS[:, b, d * P:(d + 1) * P], (HMH, HML)[k // 2][0:n, t, s], PM[0:n, t, :],
                                           start=(t == 0), stop=(t == TT - 1))
                    ins.then_inc(m_aux_in, 1)

                def turn(p):
                    b = side(4 + p)
                    pe.wait_ge(prod_made, job * 11 + (p + 1))
                    for m in range(2):
                        ins = M.transpose(PS[:, b, m * P:(m + 1) * P], SG[:, (2 * p + m) * P:(2 * p + m + 1) * P], ident)
                    ins.then_inc(m_aux_in, 1)

                pe.wait_ge(m_aux_out, job * JAUX + 4)
                for n in range(22):
                    pe.wait_ge(m_lo, job * JCH + (n + 1))
                    pe.wait_ge((gate_out, prod_made)[n % 2], job * 11 + max(n // 2 - 1, 0))
                    for k in range(KD):
                        s = slice(k * CW, (k + 1) * CW)
                        ins = three(PS[:, n % 4, 0:CW], (XEH[:, k, :], XEL[:, k, :]), (MHI[:, n % 3, s], MLO[:, n % 3, s]),
                                    k == 0, k == KD - 1)
                    ins.then_inc(m_used, 1)
                    if n % 2 and n > 1:
                        turn(n // 2 - 1)
                turn(10)
                b = side(15)
                for t in range(TT):
                    n = P if t < 2 else TS
                    ins = M.transpose(PS[:, b, t * P:t * P + n], PW[0:n, t, :], CF[0:n, C_ID:C_ID + n])
                ins.then_inc(m_aux_in, 1)
                pe.wait_ge(m_aux_out, job * JAUX + 15)
                pe.wait_ge(y_made, job)
                for n in range(22, JCH):
                    pe.wait_ge(m_lo, job * JCH + (n + 1))
                    for m in range(2):
                        kf = 2 * (n - 22) + m
                        for h in range(2):
                            s = slice(m * D + h * 512, m * D + (h + 1) * 512)
                            ins = three(PS[:, 6 + h, :], (GTH[:, kf, :], GTL[:, kf, :]), (MHI[:, n % 3, s], MLO[:, n % 3, s]),
                                        kf == 0, kf == KF - 1)
                    ins.then_inc(m_used, 1)
                pe.wait_ge(y_made, job + 1)
                pe.wait_ge(m_aux_out, job * JAUX + 16)
                for d in range(KD):
                    b = side(16 + d)
                    M.matmul(PS[:, b, 0:T], YE[:, d * P:(d + 1) * P], PTS[:, :], start=True, stop=True)\
                        .then_inc(m_aux_in, 1)

            with pe.Fori(0, NE) as job:
                job_pe(job)
            pe.wait_ge(sem("routed"), 1)
            extra = pe.value_load(XI[0:1, 4:5], min_val=0, max_val=EXTRA)
            with pe.Fori(0, EXTRA) as k:
                with pe.If(k < extra):
                    job_pe(k + NE)
            stats_pe(lambda k: SQ[:, k, :], KD, T)
            pe.wait_ge(x_ready, 4)
            for k in range(6):
                b = aux()
                n, t0 = (P if k < 4 else TS), P * (k // 2)
                for d in range(4):
                    ins = M.transpose(PS[0:n, b, d * P:(d + 1) * P], X[:, 4 * (k % 2) + d, t0:t0 + n], ident)
                ins.then_inc(aux_in, 1)


INPUTS = ["x_prompt", "x_sample", "c_prompt", "c_sample", "state_hgrn", "w_in", "gm_ln_w", "gm_ln_b", "gm_ws", "gm_bs",
          "hg_lb_raw", "hg_norm_w", "w_branch_a", "w_branch_b", "w_out", "w_ada", "b_ada", "norm_pre_mix",
          "norm_post_mix", "norm_pre_ffn", "norm_post_ffn", "w_ffn_gate", "w_ffn_up", "w_ffn_down", "w_router",
          "b_router", "w_exp_gate", "w_exp_up", "w_exp_down"]
OUTPUTS = {"yp": (1, TP, D), "ys": (NS, LS, D), "sp": (DEPTH, 1, HEADS, P, P), "ss": (DEPTH, NS, HEADS, P, P),
           "v": (DEPTH, NS, LS, D)}


def kernel(**inputs):
    import concourse.bacc as bacc
    from concourse.bass_utils import run_bass_kernel_spmd

    nc = bacc.Bacc("TRN2", target_bir_lowering=False, num_devices=1)
    arrays = {name: np.ascontiguousarray(inputs[name]) for name in INPUTS}
    arrays["const_f"], arrays["const_m"] = constants()
    aps = {name: nc.dram_tensor("in_" + name, v.shape, mybir.dt.from_np(v.dtype), kind="ExternalInput").ap()
           for name, v in arrays.items()}
    outs = {name: nc.dram_tensor("out_" + name, shape, F32, kind="ExternalOutput").ap()
            for name, shape in OUTPUTS.items()}
    build(nc, aps, outs)
    r = run_bass_kernel_spmd(nc, [{"in_" + name: v for name, v in arrays.items()}], core_ids=[0])
    return tuple(r.results[0]["out_" + name] for name in OUTPUTS)
```

```python
from contextlib import ExitStack

import numpy as np

import concourse.bass as bass
from concourse import mybir

F32 = mybir.dt.float32
F32R = mybir.dt.float32r
I32 = mybir.dt.int32
U8 = mybir.dt.uint8
U32 = mybir.dt.uint32
ALU = mybir.AluOpType
ACT = mybir.ActivationFunctionType
AX = mybir.AxisListType

P = 128
D = 1024
KD = D // P
TP = 256
NS, LS = 8, 8
TS = NS * LS
T = TP + TS
SEQS = 1 + NS
TT = 3
HEADS = 8
G4 = 4
FF = 2816
KF = FF // P
NE = 8
DEPTH = 2
EPS = 1e-6
CW = 256
LEVELS = [1, 2, 4, 8, 16, 32, 64]
ADA_TILES = 6 * KD
EXTRA = 4
JOBS = NE + EXTRA
PRODS = 2 * KF // 2
JCH = 2 * PRODS + KF
HI_RING, LO_RING = 6, 11
AHEAD = 4


def side_units():
    plan, number = {}, 0
    for c in range(JCH):
        units = []
        n = c // 2 if c % 2 and c < 2 * PRODS else None
        if n is not None and n < KD:
            units.append(("combine", n))
        if n is not None and n % 2 and n > 1:
            units.append(("turn", n // 2 - 1))
        if n == PRODS - 1:
            units += [("turn", 10), ("place", 0)]
        if c - 2 * PRODS in (2, 6, 10, 14):
            units.append(("gather", (c - 2 * PRODS) // 4))
        plan[c] = [(number + i, what, k) for i, (what, k) in enumerate(units)]
        number += len(units)
    return plan, number


SIDE, JAUX = side_units()
PLACE = next(s for units in SIDE.values() for s, what, _ in units if what == "place")

PARTS = ["f", "q", "i", "v", "u", "g", "A", "ga", "gb", "B", "O"]
COL = {"u": 0, "v": 1024, "q": 2048, "f": 3072, "i": 4096, "g": 5120, "ga": 6144, "gb": 7168}
BASE = {}
for _l in range(DEPTH):
    for _n, _p in enumerate(PARTS):
        BASE[_l, _p] = _l * 82 + 4 * _n
GU_BASE, DOWN_BASE = 44, 66
CHUNKS = 82 + 44
ADA_FIRST = 2 * KD

C_ID, C_IOTA, C_TRI, C_UPPER, C_SEQ, C_IOTA8, C_N = 0, 128, 256, 384, 512, 520, 528


def constants():
    c = np.zeros((P, C_N), np.float32)
    i = np.arange(P)
    c[:, C_ID:C_ID + P] = np.eye(P)
    c[:, C_IOTA:C_IOTA + P] = i[None, :]
    c[:, C_TRI:C_TRI + P] = i[:, None] < i[None, :]
    c[:, C_UPPER:C_UPPER + P] = i[:, None] <= i[None, :]
    c[:TS, C_SEQ:C_SEQ + NS] = i[:TS, None] // LS == np.arange(NS)[None, :]
    c[:, C_IOTA8:C_IOTA8 + 8] = np.arange(8)[None, :]
    m = np.zeros((P, 1 + len(LEVELS), P), np.float32)
    m[:, 0] = np.eye(P)
    s, t = i[:, None], i[None, :]
    for n, b in enumerate(LEVELS):
        m[:, n + 1] = (s // (2 * b) == t // (2 * b)) & (s // b % 2 == 0) & (t // b % 2 == 1)
    return c, m


class Seen:

    def __init__(self, eng):
        self.eng, self.n = eng, {}

    def next(self, sem):
        self.n[id(sem)] = self.n.get(id(sem), 0) + 1
        self.eng.wait_ge(sem, self.n[id(sem)])

    def note(self, ins, sem):
        ins.then_inc(sem, 1)
        self.n[id(sem)] = self.n.get(id(sem), 0) + 1
        return self.n[id(sem)]

    def step(self, ins, sem):
        ins.then_inc(sem, 1)
        self.next(sem)


def build(nc, a, out):
    ctx = ExitStack()
    with ctx:
        sems = {}

        def sem(name):
            if name not in sems:
                sems[name] = ctx.enter_context(nc.semaphore(name))
            return sems[name]

        low = (nc.sbuf_base + 31) // 32 * 32

        def at(name, shape, dt, offset):
            return nc.alloc_sbuf_tensor_at(name, shape, dt, offset=low + offset, align_bytes=16)

        RING = 0
        O_X = 73728
        O_H1 = O_X + 10240
        HLB = 4 * (KD * T + 64)
        O_H2 = O_H1 + 2 * HLB
        O_F = O_H2 + 2 * HLB
        O_Q = O_F + 12288
        O_K = O_Q + 10240
        O_I = O_K + 10240
        O_V = O_I + 12288
        O_A = O_V + 12288
        O_M = O_A + 10240
        RAW = at("raw", [P, 2, KD * CW], F32, RING)
        WHI = at("whi", [P, 2, KD * CW], F32R, RING + 16384)
        WLO = at("wlo", [P, 2, KD * CW], F32R, RING + 32768)
        FIRST = at("first", [P, 4, KD * CW], F32, RING + 16384)
        ADA = at("ada", [P, 2, KD, P], F32, RING + 49152)
        SC = at("sc", [P, 2560], F32, RING + 57344)
        WST = at("wst", [P, G4, P], F32, RING + 67584)
        WSS = at("wss", [TS, G4, TS], F32, RING + 69632)
        T2 = at("t2", [P, 2, T], F32, RING + 70656)
        MHI = at("mhi", [P, HI_RING, D], F32R, RING)
        MRAW = at("mraw", [P, LO_RING, D], F32, RING + 4 * D * HI_RING)
        MLO = at("mlo", [P, LO_RING, D], F32R, RING + 4 * D * HI_RING)
        X = at("x", [P, KD, T], F32, O_X)
        H1H = at("h1h", [P, KD * T + 64], F32R, O_H1)
        H1L = at("h1l", [P, KD * T + 64], F32R, O_H1 + HLB)
        H2H = at("h2h", [P, KD * T + 64], F32R, O_H2)
        H2L = at("h2l", [P, KD * T + 64], F32R, O_H2 + HLB)
        LNW = at("lnw", [P, D], F32, O_H2)
        LNB = at("lnb", [P, D], F32, O_H2 + 4096)
        WSR = at("wsr", [P, G4, P], F32, O_H2 + 8192)
        WSRS = at("wsrs", [TS, G4, TS], F32, O_H2 + HLB)
        GB = at("gb", [P, KD, T], F32, O_H2 + HLB)
        FG = at("fg", [P, HEADS, T], F32, O_F)
        KTM = at("ktm", [P, TT, D], F32, O_F)
        OT = at("ot", [P, 512], F32, O_F)
        OSQ = at("osq", [P, 512], F32, O_F + 2048)
        ON = at("on", [P, 512], F32, O_F + 4096)
        HT = at("ht", [P, KD, T], F32, O_Q)
        QQ = at("qq", [P, HEADS, T], F32, O_Q)
        KK = at("kk", [P, HEADS, T], F32, O_K)
        ST = at("st", [P, 2, HEADS, P], F32, O_K)
        STB = at("stb", [P, 2, HEADS, P], F32, O_H2)
        IT = at("it", [P, TT, D], F32, O_I)
        VT = at("vt", [P, TT, D], F32, O_V)
        GS = at("gs", [P, KD, T], F32, O_V)
        SA = at("sa", [P, KD, T], F32, O_A)
        BA = at("ba", [P, 1280], F32, O_A)
        BB = at("bb", [P, 640], F32, O_A + 5120)
        IM = at("im", [TS, 2, D], F32, RING + 57344)
        PRH = at("prh", [P, KF, T], F32R, O_F)
        PRL = at("prl", [P, KF, T], F32R, O_F + 4 * KF * T)
        XTM = at("xtm", [P, TT, D], F32, O_I)
        CT = at("ct", [SEQS, D], F32, O_Q)
        VR = at("vr", [P, 2, P], F32, O_K)
        HMH = at("hmh", [P, TT, D], F32R, O_H1)
        HML = at("hml", [P, TT, D], F32R, O_H1 + 12288)
        XEH = at("xeh", [P, KD, P], F32R, O_H1 + 24576)
        XEL = at("xel", [P, KD, P], F32R, O_H1 + 28672)
        PM = at("pm", [P, TT, P], F32R, O_H1 + 32768)
        PW = at("pw", [P, TT, P], F32, O_H1 + 34304)
        PTS = at("pts", [P, T], F32, O_H1 + 35840)
        YE = at("ye", [P, D], F32, O_H1 + 37120)
        SG = at("sg", [P, FF], F32, O_F)
        GTH = at("gth", [P, KF, P], F32R, O_F + 11264)
        GTL = at("gtl", [P, KF, P], F32R, O_F + 22528)
        WR = at("wr", [P, KD, NE], F32, O_V)
        BR = at("br", [P, NE], F32, O_V + 256)
        R0 = O_V + 512
        LG = at("lg", [P, TT, NE], F32, R0)
        TOPV = at("topv", [P, TT, 8], F32, R0 + 96)
        TOPI = at("topi", [P, TT, 8], U32, R0 + 192)
        TOPF = at("topf", [P, TT, 2], F32, R0 + 288)
        S1 = at("s1", [P, TT, NE], F32, R0 + 320)
        S2 = at("s2", [P, TT, NE], F32, R0 + 416)
        SEL = at("sel", [P, TT, NE], F32, R0 + 512)
        WT = at("wt", [P, TT, NE], F32, R0 + 608)
        PR = at("pr", [P, TT, 4], F32, R0 + 704)
        POS = at("pos", [P, TT, NE], F32, R0 + 768)
        CNT = at("cnt", [P, 8, NE], F32, R0 + 864)
        POSJ = at("posj", [P, TT, JOBS + 1], F32, R0 + 1184)
        WJ = at("wj", [P, TT, JOBS + 1], F32, R0 + 1376)
        OH = at("oh", [P, 3, NE], F32, R0 + 1568)
        JT = at("jt", [P, TT, NE], F32, R0 + 1696)
        XI = at("xi", [1, 8], I32, R0 + 1824)
        XF = at("xf", [P, 8], F32, R0 + 1856)
        o = O_M
        CF = at("cf", [P, C_N], F32, o)
        CM = at("cm", [P, 8, P], U8, o + 2112)
        ONES = at("ones", [P, P], F32, o + 3136)
        MOD = at("mod", [P, 2 * ADA_TILES, SEQS], F32, o + 3648)
        VEC = at("vec", [P, 2, P], F32, o + 7104)
        CS = at("cs", [P, KD, SEQS], F32, o + 8128)
        RST = at("rst", [P, 512], F32, o + 8416)
        RSTD = at("rstd", [P, 512], F32, o + 10464)
        AM = at("am", [P, KD, SEQS], F32, o + 12512)
        LB = at("lb", [P, DEPTH, KD], F32, o + 12800)
        OML = at("oml", [P, DEPTH, KD], F32, o + 12864)
        LT = at("lt", [P, 3, KD], F32, o + 12928)
        BP = at("bp", [P, HEADS, 2], F32, o + 13024)
        BS = at("bs", [P, HEADS, NS], F32, o + 13088)
        BN = at("bn", [P, TT, 12], F32, o + 13344)
        MV = at("mv", [P, TT, 4], F32, o + 13488)
        T1 = at("t1", [P, 2, 2, T], F32, o + 13536)
        BGS = at("bgs", [P, T], F32, O_A + 7680)
        assert low + o + 18656 <= nc.sbuf_usable_end, (low + o + 18656, nc.sbuf_usable_end)

        PS = ctx.enter_context(nc.psum_tensor("ps", [P, 8, 512], F32))
        ident = CF[:, C_ID:C_ID + P]

        wide = {}
        for l in range(DEPTH):
            for p in PARTS:
                src = {"A": a["w_branch_a"], "B": a["w_branch_b"], "O": a["w_out"]}.get(p, a["w_in"])
                wide[l, p] = (src[l].rearrange("(k p) n -> p k n", p=P), COL.get(p, 0))
        ada_src = [a["w_ada"][l].rearrange("(k p) n -> p k n", p=P) for l in range(DEPTH)]
        gate_src = a["w_ffn_gate"][0].rearrange("(k p) n -> p k n", p=P)
        up_src = a["w_ffn_up"][0].rearrange("(k p) n -> p k n", p=P)
        down_src = a["w_ffn_down"][0].rearrange("(k p) n -> p k n", p=P)

        raw_in = [sem("raw_in0"), sem("raw_in1")]
        hi_made, lo_made = sem("hi_made"), sem("lo_made")
        chunk_used = sem("chunk_used")
        psum_out = sem("psum_out")
        ada_in = [sem("ada_in0"), sem("ada_in1")]
        ada_used, ada_made = sem("ada_used"), sem("ada_made")
        aux_in, aux_out = sem("aux_in"), sem("aux_out")
        sq_made, sq_used, ms_made, std_made = sem("sq_made"), sem("sq_used"), sem("ms_made"), sem("std_made")
        dve_step = sem("dve_step")
        x_ready = sem("x_ready")
        operand = sem("operand")
        m_raw = [sem(f"m_raw{n}") for n in range(LO_RING)]
        m_hi, m_lo, m_used = sem("m_hi"), sem("m_lo"), sem("m_used")
        gate_out, prod_made, y_made = sem("gate_out"), sem("prod_made"), sem("y_made")
        m_aux_in, m_aux_out, p_made, gt_hi = sem("m_aux_in"), sem("m_aux_out"), sem("p_made"), sem("gt_hi")

        def through(eng, base, n, body, loop=True):
            if loop and base:
                with eng.Fori(0, n // 2) as i:
                    for j in range(2):
                        body(i * 2 + (base + j), i + base // 2, j, i * 2 + j)
            else:
                for k in range(n):
                    body(base + k, (base + k) // 2, k % 2, k)

        def hm_unit(t, k, number):
            n = P if k < 4 else TS
            return t[0:n, k // 2, 512 * (k % 2):512 * (k % 2) + 512], PS[0:n, 4 + number % 2, :]

        def states_stored(eng, l):
            eng.wait_ge(sem("sp_stored"), 16 * (l + 1))
            for n in range(4):
                eng.wait_ge(sem(f"st_stored{n}"), 16 * 2 * (l + 1))

        def state(s):
            return ((STB, ST)[s % 4 // 2][:, s % 2], s % 4)

        def square_slot(n):
            return T1[:, n % 4 // 2, n % 2, :]

        def first_ada(n):
            return FIRST[:, n % 4, :].rearrange("p (k n) -> p k n", k=KD)

        mark = {}

        block = ctx.enter_context(nc.Block())

        @block.sync
        def _(sp):
            def load_raw(c, j, src, cols=KD * CW):
                if not (isinstance(c, int) and c < 2):
                    sp.wait_ge(lo_made, c - 1)
                sp.dma_start(RAW[:, j, 0:cols].rearrange("p (k n) -> p k n", k=src.shape[1]),
                             src).then_inc(raw_in[j], 16)

            def load_ada(t, j, l, col):
                if not (isinstance(t, int) and t < ADA_FIRST + 2):
                    sp.wait_ge(ada_used, t - 1)
                sp.dma_start(ADA[:, j], ada_src[l][:, :, bass.ds(col, P)]).then_inc(ada_in[j], 16)

            for n in range(ADA_FIRST // 2):
                if n >= 4:
                    sp.wait_ge(ada_used, 2 * (n - 4) + 2)
                sp.dma_start(first_ada(n), ada_src[0][:, :, n * CW:(n + 1) * CW]).then_inc(sem(f"first_in{n % 4}"), 16)
                if n in (3, 4):
                    src, c0 = wide[0, "f"]
                    load_raw(n - 3, n - 3, src[:, :, c0 + (n - 3) * CW:c0 + (n - 2) * CW])

            for l in range(DEPTH):
                for p in PARTS:
                    src, c0 = wide[l, p]
                    base = BASE[l, p]

                    def one(c, r, j, n):
                        if not (isinstance(c, int) and c < 2):
                            load_raw(c, j, src[:, :, bass.ds(n * CW + c0, CW)])
                        if l == 0:
                            al, first = (0, ADA_FIRST + base) if base < 32 else (1, base - 32)
                            load_ada(c + ADA_FIRST, j, al, (n + first) * P)
                    through(sp, base, 4, one, loop=(base > 0))
                if l == 0:
                    with sp.Fori(0, 11) as i:
                        for j, src in enumerate((gate_src, up_src)):
                            load_raw(i * 2 + (GU_BASE + j), j, src[:, :, bass.ds(i * CW, CW)])
                            load_ada(i * 2 + (GU_BASE + j + ADA_FIRST), j, 1, (i * 2 + (12 + j)) * P)
                    def down(i, ada):
                        for j in range(2):
                            load_raw(i * 2 + (DOWN_BASE + j), j, down_src[:, 11 * j:11 * j + 11, bass.ds(i * P, P)],
                                     11 * P)
                            if ada:
                                load_ada(i * 2 + (DOWN_BASE + j + ADA_FIRST), j, 1, (i * 2 + (34 + j)) * P)
                    with sp.Fori(0, 7) as i:
                        down(i, True)
                    down(7, False)

            wg, wu, wd = (a[k][0] for k in ("w_exp_gate", "w_exp_up", "w_exp_down"))

            def load_job(job, e, first=False):
                g = wg[bass.ds(e, 1)].rearrange("e (k p) n -> p (e k) n", p=P)
                u = wu[bass.ds(e, 1)].rearrange("e (k p) n -> p (e k) n", p=P)
                d = wd[bass.ds(e, 1)].rearrange("e (k p) n -> p (e k) n", p=P)
                for c in range(JCH):
                    if not (first and c < LO_RING - 2):
                        sp.wait_ge(m_used, job * JCH + (c - LO_RING + 3))
                    if c < 2 * PRODS:
                        n, k = c // 2, 4 * (c % 2)
                        src = (g, u)[n % 2][:, k:k + 4, (n // 2) * CW:(n // 2 + 1) * CW]
                    else:
                        src = d[:, c - 2 * PRODS:c - 2 * PRODS + 1, :]
                    sp.dma_start(MRAW[:, c % LO_RING, :].rearrange("p (k n) -> p k n", k=src.shape[1]),
                                 src).then_inc(m_raw[c % LO_RING], 16)

            sp.wait_ge(chunk_used, CHUNKS)
            sp.wait_ge(psum_out, CHUNKS)
            load_job(0, 0, first=True)
            with sp.Fori(1, NE) as job:
                load_job(job, job)
            sp.wait_ge(sem("routed"), 1)
            extra = sp.value_load(XI[0:1, 4:5], min_val=0, max_val=EXTRA)
            with sp.Fori(0, EXTRA) as k:
                with sp.If(k < extra):
                    e = sp.value_load(XI[0:1, bass.ds(k, 1)], min_val=0, max_val=NE - 1)
                    load_job(k + NE, e)
            for c in range(HI_RING):
                sp.wait_ge(m_used, extra * JCH + (NE * JCH + c - LO_RING + 3))
                sp.dma_start(MRAW[:, c, :], wg[0, 0:P, 0:D]).then_inc(m_raw[c], 16)

        @block.vector
        def _(dve):
            see = Seen(dve)
            V = nc.vector

            def lo(c, r, j):
                if isinstance(c, int) and c >= CHUNKS:
                    return
                if isinstance(c, int) and c < 2:
                    dve.wait_ge(ada_used, 14 + 2 * c)
                dve.wait_ge(hi_made, c + 1)
                V.tensor_tensor(WLO[:, j, :], RAW[:, j, :], WHI[:, j, :].bitcast(F32),
                                ALU.subtract).then_inc(lo_made, 1)

            def ada_out(t):
                dve.wait_ge(ada_used, t + 1)
                V.tensor_scalar(MOD[:, bass.ds(t, 1), :], PS[:, 7:8, 0:SEQS], VEC[:, 0, bass.ds(t, 1)], None,
                                ALU.add).then_inc(ada_made, 1)

            def after(l, c, r, j):
                lo(c + 2, r + 1, j)
                if l == 0:
                    ada_out(c + ADA_FIRST)

            x = [0]

            def aux():
                see.next(aux_in)
                x[0] += 1
                return 4 + (x[0] - 1) % 2

            def st(ins):
                see.step(ins, dve_step)

            def v3(t):
                return t[:, 0:KD * T].rearrange("p (k t) -> p k t", k=KD)

            nsq = [0]

            def stats_dve(n, size, tiles):
                nsq[0] += tiles
                dve.wait_ge(sq_used, nsq[0])
                V.tensor_scalar(RST[:, 0:n], PS[:, 6, 0:n], 1.0 / size, EPS, ALU.mult, ALU.add).then_inc(ms_made, 1)
                see.next(std_made)
                st(V.reciprocal(RSTD[:, 0:n], RST[:, 0:n]))

            rb = RSTD[:, 0:TP]
            rb_samples = RSTD[:, TP:T].unsqueeze(1).broadcast_to([P, KD, TS])

            def seq(m):
                return m[:, :, 1:SEQS].unsqueeze(3).broadcast_to([P, KD, NS, LS])

            def samples(t):
                return t[:, :, TP:T].rearrange("p k (s t) -> p k s t", s=NS)

            def pre_norm_dve(l, w, sh, sc, parts, with_stats=True):
                if with_stats:
                    dve.wait_ge(x_ready, see.n[id(x_ready)])
                dve.wait_ge(ada_made, sc + KD)
                st(V.scalar_tensor_tensor(AM[:, :, :], MOD[:, sc:sc + KD, :], 1.0,
                                          VEC[:, 1, w + 8 * l:w + 8 * l + 8].unsqueeze(2).broadcast_to([P, KD, SEQS]),
                                          ALU.add, ALU.mult))
                if with_stats:
                    stats_dve(T, D, KD)
                st(V.tensor_tensor(HT[:, :, TP:T], X[:, :, TP:T], rb_samples, ALU.mult))
                st(V.tensor_tensor(samples(HT), samples(HT), seq(AM), ALU.mult))
                see.step(V.tensor_tensor(samples(HT), samples(HT), seq(MOD[:, sh:sh + KD, :]), ALU.add),
                         sem("hs_made"))

                def low(d):
                    dve.wait_ge(sem("xr_made"), made[d])
                    see.next(sem("h_hi"))
                    V.scalar_tensor_tensor(v3(parts[1])[:, d, 0:TP], HT[:, d, 0:TP], MOD[:, sh + d, 0:1],
                                           v3(parts[0])[:, d, 0:TP].bitcast(F32), ALU.add, ALU.subtract)\
                        .then_inc(operand, 1)

                made = []
                for d in range(KD):
                    made.append(see.note(V.scalar_tensor_tensor(HT[:, d, 0:TP], X[:, d, 0:TP], AM[:, d, 0:1], rb,
                                                                ALU.mult, ALU.mult), sem("xr_made")))
                    if parts is None:
                        continue
                    if d == 1:
                        see.next(sem("h_hi"))
                        V.tensor_tensor(v3(parts[1])[:, :, TP:T], HT[:, :, TP:T], v3(parts[0])[:, :, TP:T].bitcast(F32),
                                        ALU.subtract)
                    if d >= 1:
                        low(d - 1)
                if parts is not None:
                    low(KD - 1)

            def post_norm_dve(l, w, g):
                st(V.tensor_tensor(AM[:, :, :], MOD[:, g:g + KD, :],
                                   VEC[:, 1, w + 8 * l:w + 8 * l + 8].unsqueeze(2).broadcast_to([P, KD, SEQS]),
                                   ALU.mult))
                stats_dve(T, D, KD)
                st(V.tensor_tensor(SA[:, :, TP:T], SA[:, :, TP:T], rb_samples, ALU.mult))
                st(V.tensor_tensor(samples(SA), samples(SA), seq(AM), ALU.mult))
                V.tensor_tensor(X[:, :, TP:T], X[:, :, TP:T], SA[:, :, TP:T], ALU.add)
                made = []
                for d in range(KD + 1):
                    if d < KD:
                        made.append(see.note(V.scalar_tensor_tensor(SA[:, d, 0:TP], SA[:, d, 0:TP], AM[:, d, 0:1], rb,
                                                                    ALU.mult, ALU.mult), dve_step))
                    if d:
                        dve.wait_ge(dve_step, made[d - 1])
                        see.note(V.tensor_tensor(X[:, d - 1, 0:TP], X[:, d - 1, 0:TP], SA[:, d - 1, 0:TP], ALU.add),
                                 x_ready)

            for k in range(5):
                b = aux()
                if k < 4:
                    t, h = k // 2, k % 2
                    V.tensor_copy(X[:, 4 * h:4 * h + 4, t * P:(t + 1) * P],
                                  PS[:, b, :].rearrange("p (k t) -> p k t", k=4)).then_inc(aux_out, 1)
                else:
                    V.tensor_copy(X[:, :, TP:T], PS[:, b, :].rearrange("p (k t) -> p k t", k=KD)).then_inc(aux_out, 1)
            dve.wait_ge(aux_out, 5)
            b = aux()
            V.tensor_copy(VEC[:, 0, 0:96], PS[:, b, 0:96])
            V.tensor_copy(VEC[:, 1, 0:82], PS[:, b, P:P + 82]).then_inc(aux_out, 1)
            b = aux()
            V.tensor_copy(CS[:, :, :], PS[:, b, 0:P].rearrange("p (k t) -> p k t", k=KD)[:, :, 0:SEQS])\
                .then_inc(aux_out, 1)
            dve.wait_ge(aux_out, 7)
            lb0, lb1 = VEC[:, 1, 64:72], VEC[:, 1, 72:80]
            st(V.tensor_tensor(LT[:, 2, :], lb0, lb1, ALU.max))
            V.tensor_tensor(LT[:, 0:2, :], VEC[:, 1, 64:80].rearrange("p (l k) -> p l k", l=2),
                            LT[:, 2:3, :].broadcast_to([P, 2, KD]), ALU.subtract).then_inc(sem("lb_shifted"), 1)
            see.next(sem("lb_exp"))
            st(V.tensor_tensor(LT[:, 2, :], LT[:, 0, :], LT[:, 1, :], ALU.add))
            st(V.reciprocal(LT[:, 2, :], LT[:, 2, :]))
            st(V.tensor_tensor(LT[:, 0:2, :], LT[:, 0:2, :], LT[:, 2:3, :].broadcast_to([P, 2, KD]), ALU.mult))
            st(V.tensor_tensor(LT[:, 1, :], LT[:, 0, :], LT[:, 1, :], ALU.add))
            st(V.tensor_tensor(LB[:, :, :], LT[:, 0:2, :], LT[:, 0:1, :].broadcast_to([P, 2, KD]), ALU.subtract))
            st(V.tensor_scalar(OML[:, :, :], LB[:, :, :], -1.0, 1.0, ALU.mult, ALU.add))
            stats_dve(T, D, KD)
            for t in range(ADA_FIRST):
                ada_out(t)
            lo(0, 0, 0)
            lo(1, 0, 1)

            for l in range(DEPTH):
                def only(c, r, j, n):
                    after(l, c, r, j)

                pre_norm_dve(l, 0, ADA_TILES * l, ADA_TILES * l + 8, (H1H, H1L), with_stats=(l > 0))
                through(dve, BASE[l, "f"], 4, only)
                dve.wait_ge(psum_out, BASE[l, "f"] + 4)
                for h in range(HEADS):
                    V.tensor_scalar(FG[:, h, :], FG[:, h, :], OML[:, l, h:h + 1], LB[:, l, h:h + 1], ALU.mult, ALU.add)
                    ins = V.tensor_scalar(KK[:, h, :], KK[:, h, :], OML[:, l, h:h + 1], None, ALU.mult)
                ins.then_inc(sem("k_ready"), 1)
                see.next(sem("k_ready"))
                through(dve, BASE[l, "q"], 4, only)
                through(dve, BASE[l, "i"], 4, only)

                def scores(level, units):
                    for k in range(units):
                        b = aux()
                        if k < 4:
                            src = PS[:, b, :].rearrange("p (h t) -> p h t", h=4)
                            dst = SC[:, k * 512:(k + 1) * 512].rearrange("p (h t) -> p h t", h=4)
                            m = CM[:, level:level + 1, :].broadcast_to([P, 4, P])
                        else:
                            src = PS[0:TS, b, :].rearrange("p (h t) -> p h t", h=8)
                            dst = SC[0:TS, 2048:2560].rearrange("p (h t) -> p h t", h=8)
                            m = CM[0:TS, level:level + 1, 0:TS].broadcast_to([TS, 8, TS])
                        V.copy_predicated(dst, m, src).then_inc(aux_out, 1)
                        dve.wait_ge(aux_out, x[0])

                def level_scores(n):
                    scores(n + 1, 5 if LEVELS[n] < LS else 4)

                def level(n):
                    m = LEVELS[n]
                    toks = T if m < LS else TP
                    nb = toks // (2 * m)
                    cur = FG if n == 0 else (BA, BB)[(n - 1) % 2]
                    nxt = (BA, BB)[n % 2]
                    if n == 0:
                        c4 = FG[:, :, :].rearrange("p h (b two) -> p h b two", two=2)
                    else:
                        c4 = cur[:, 0:HEADS * (toks // m)].rearrange("p (h b two) -> p h b two", h=HEADS, two=2)
                    q5 = QQ[:, :, 0:toks].rearrange("p h (b two m) -> p h b two m", two=2, m=m)
                    k5 = KK[:, :, 0:toks].rearrange("p h (b two m) -> p h b two m", two=2, m=m)
                    shape = [P, HEADS, nb, m]

                    def each(t5, half, b4):
                        bc = b4.unsqueeze(3).broadcast_to(shape)
                        return V.tensor_tensor(t5[:, :, :, half, :], t5[:, :, :, half, :], bc, ALU.mult)
                    each(q5, 1, c4[:, :, :, 0])
                    st(each(k5, 0, c4[:, :, :, 1]))
                    if m == LS // 2:
                        p4 = cur[:, 0:HEADS * (T // m)].rearrange("p (h b two) -> p h b two", h=HEADS, two=2)
                        V.tensor_tensor(BS[:, :, :], p4[:, :, TP // LS:, 0], p4[:, :, TP // LS:, 1], ALU.mult)
                        p4 = p4[:, :, 0:TP // LS, :]
                        nbo = TP // LS
                    else:
                        p4, nbo = c4, nb
                    if m == LEVELS[-1]:
                        ins = V.tensor_tensor(BP[:, :, :], p4[:, :, :, 0], p4[:, :, :, 1], ALU.mult)
                    else:
                        ins = V.tensor_tensor(nxt[:, 0:HEADS * nbo].rearrange("p (h b) -> p h b", h=HEADS),
                                              p4[:, :, :, 0], p4[:, :, :, 1], ALU.mult)
                    ins.then_inc(sem("level_made"), 1)
                    see.next(sem("level_made"))

                dve.wait_ge(psum_out, BASE[l, "i"] + 4)
                see.next(sem("sc_zero"))
                if l == 0:
                    dve.wait_ge(sem("mask_made"), 1)
                for k in range(4):
                    c = BASE[l, "v"] + k
                    if k == 0:
                        scores(0, 5)
                    else:
                        level_scores(k - 1)
                    after(l, c, c // 2, k % 2)
                    if k == 0:
                        see.step(V.tensor_tensor(QQ[:, :, :], QQ[:, :, :], FG[:, :, :], ALU.mult), sem("level_made"))
                    else:
                        level(k - 1)
                dve.wait_ge(psum_out, BASE[l, "v"] + 4)
                for t in range(TT):
                    n = P if t < 2 else TS
                    for h in range(2):
                        ins = V.bn_stats(BN[0:n, t, 6 * h:6 * h + 6], VT[0:n, t, 512 * h:512 * h + 512])
                st(ins)
                for t in range(TT):
                    n = P if t < 2 else TS
                    ins = V.bn_aggr(MV[0:n, t, 0:2], BN[0:n, t, :])
                st(ins)
                if l == 0:
                    st(V.memset(MV[TS:P, 2, :], 1.0))
                V.tensor_scalar(MV[:, :, 2:3], MV[:, :, 1:2], EPS, None, ALU.add).then_inc(sem("var_made"), 1)
                see.next(sem("vstd_made"))
                st(V.reciprocal(MV[:, :, 3:4], MV[:, :, 2:3]))
                dve.wait_ge(sem("ln_in"), 32 * (l + 1))
                for t in range(TT):
                    n = P if t < 2 else TS
                    ins = V.tensor_scalar(VT[0:n, t, :], VT[0:n, t, :], MV[0:n, t, 0:1], MV[0:n, t, 3:4],
                                          ALU.subtract, ALU.mult)
                st(ins)
                for t in range(TT):
                    n = P if t < 2 else TS
                    ins = V.tensor_tensor(VT[0:n, t, :], VT[0:n, t, :], LNW[0:n, :], ALU.mult)
                st(ins)
                for t in range(TT):
                    n = P if t < 2 else TS
                    ins = V.tensor_tensor(VT[0:n, t, :], VT[0:n, t, :], LNB[0:n, :], ALU.add)
                ins.then_inc(sem("v_ready"), 1)
                see.next(sem("v_ready"))
                b = aux()
                V.tensor_tensor(WST[:, :, :], PS[:, b, :].rearrange("p (g t) -> p g t", g=G4),
                                CF[:, C_UPPER:C_UPPER + P].unsqueeze(1).broadcast_to([P, G4, P]), ALU.mult)\
                    .then_inc(aux_out, 1)
                b = aux()
                V.tensor_tensor(WSS[:, :, :], PS[0:TS, b, 0:G4 * TS].rearrange("p (g t) -> p g t", g=G4),
                                CF[0:TS, C_UPPER:C_UPPER + TS].unsqueeze(1).broadcast_to([TS, G4, TS]), ALU.mult)\
                    .then_inc(aux_out, 1)
                for k in range(4):
                    c = BASE[l, "u"] + k
                    dve.wait_ge(psum_out, c + 1)
                    if k:
                        see.next(sem("a_lo"))
                    see.next(sem("mixed"))
                    see.step(V.tensor_tensor(T2[:, :, :], T1[:, 0], PS[:, 4:6, 0:T], ALU.mult), sem("a_made"))
                    see.next(sem("a_hi"))
                    V.tensor_tensor(v3(H2L)[:, 2 * k:2 * k + 2, :], T2[:, :, :],
                                    v3(H2H)[:, 2 * k:2 * k + 2, :].bitcast(F32), ALU.subtract).then_inc(sem("a_lo"), 1)
                    if k in (1, 3):
                        level_scores(3 + k // 2)
                    lo(c + 2, (c + 2) // 2, k % 2)
                    if l == 0:
                        ada_out(c + ADA_FIRST)
                    if k in (1, 3):
                        level(3 + k // 2)
                see.next(sem("a_lo"))
                for k in range(4):
                    c = BASE[l, "g"] + k
                    if k in (1, 3):
                        level_scores(5 + k // 2)
                    after(l, c, c // 2, k % 2)
                    if k in (1, 3):
                        level(5 + k // 2)
                for k in range(4):
                    c = BASE[l, "A"] + k
                    if k == 0:
                        for n in range(4):
                            b = aux()
                            V.tensor_copy(KTM[:, n // 2, 512 * (n % 2):512 * (n % 2) + 512],
                                          PS[:, b, :]).then_inc(aux_out, 1)
                        for n in range(2):
                            b = aux()
                            V.tensor_copy(KTM[0:TS, 2, 512 * n:512 * n + 512], PS[0:TS, b, :]).then_inc(aux_out, 1)
                    if k == 1:
                        for n in range(2):
                            b = aux()
                            V.tensor_copy(ST[:, 0, 4 * n:4 * n + 4, :],
                                          PS[:, b, :].rearrange("p (h v) -> p h v", h=4)).then_inc(aux_out, 1)
                        dve.wait_ge(aux_out, x[0])
                    if k == 2:
                        for n in range(2):
                            b = aux()
                            for h in range(4):
                                ins = V.scalar_tensor_tensor(ST[:, 1, 4 * n + h, :], ST[:, 0, 4 * n + h, :],
                                                             BP[:, 4 * n + h, 1:2], PS[:, b, h * P:(h + 1) * P],
                                                             ALU.mult, ALU.add)
                            ins.then_inc(aux_out, 1)
                        dve.wait_ge(aux_out, x[0])
                        mark["s2", l] = x[0]
                    after(l, c, c // 2, k % 2)

                def o_norm(dst, g):
                    stats_dve(512, P, 1)
                    st(V.tensor_tensor(ON[:, :], OT[:, :], RSTD[:, :], ALU.mult))
                    v = ON[:, :].rearrange("p (h t) -> p h t", h=dst.shape[1])
                    see.step(V.scalar_tensor_tensor(dst, v, VEC[:, 1, 80 + l:81 + l], g, ALU.mult, ALU.mult),
                             sem("on_made"))

                def prompt_norm(k):
                    o_norm(HT[:, 2 * k:2 * k + 2, 0:TP], GS[:, 2 * k:2 * k + 2, 0:TP])

                for k in range(4):
                    c = BASE[l, "ga"] + k
                    after(l, c, c // 2, k % 2)
                    dve.wait_ge(psum_out, c + 1)
                    see.step(V.tensor_tensor(SA[:, 2 * k:2 * k + 2, :], SA[:, 2 * k:2 * k + 2, :], T1[:, 1],
                                             ALU.mult), sem("ga_used"))
                    if k:
                        prompt_norm(k - 1)
                    b = aux()
                    V.tensor_copy(OT[:, :], PS[:, b, :]).then_inc(aux_out, 1)
                    dve.wait_ge(aux_out, x[0])
                    mark["o", l, k] = x[0]
                for k in range(4):
                    c = BASE[l, "gb"] + k
                    if k == 0:
                        prompt_norm(3)
                    after(l, c, c // 2, k % 2)
                    for s in (2 * k, 2 * k + 1):
                        old, _ = state(s)
                        dve.wait_ge(sem("st_read"), 8 * l + s + 1)
                        for n in range(2):
                            b = aux()
                            for h in range(4 * n, 4 * n + 4):
                                ins = V.scalar_tensor_tensor(old[:, h, :], old[:, h, :], BS[:, h, s:s + 1],
                                                             PS[:, b, (h % 4) * P:(h % 4 + 1) * P], ALU.mult, ALU.add)
                            ins.then_inc(aux_out, 1)
                        mark["st", l, s] = x[0]
                        if k == 3:
                            for d in range(4 * (s % 2), 4 * (s % 2) + 4, 2):
                                see.next(sem("h_hi"))
                                V.tensor_tensor(v3(H1L)[:, d:d + 2, 0:TP], HT[:, d:d + 2, 0:TP],
                                                v3(H1H)[:, d:d + 2, 0:TP].bitcast(F32), ALU.subtract)
                dve.wait_ge(sem("st_read"), 8 * l + 8)
                see.step(V.tensor_copy(OT[:, :], PS[:, 6, :]), sem("os_out"))
                o_norm(HT[:, :, TP:T], GS[:, :, TP:T])
                see.next(sem("h_hi"))
                V.tensor_tensor(v3(H1L)[:, :, TP:T], HT[:, :, TP:T], v3(H1H)[:, :, TP:T].bitcast(F32),
                                ALU.subtract).then_inc(operand, 1)
                for k in range(4):
                    c = BASE[l, "B"] + k
                    after(l, c, c // 2, k % 2)
                    dve.wait_ge(psum_out, c + 1)
                    st(V.tensor_tensor(T2[:, :, :], T1[:, 0], GB[:, 2 * k:2 * k + 2, :], ALU.mult))
                    see.step(V.tensor_tensor(SA[:, 2 * k:2 * k + 2, :], SA[:, 2 * k:2 * k + 2, :], T2[:, :, :],
                                             ALU.add), sem("merged"))
                    see.next(sem("merged_hi"))
                    V.tensor_tensor(v3(H2L)[:, 2 * k:2 * k + 2, :], SA[:, 2 * k:2 * k + 2, :],
                                    v3(H2H)[:, 2 * k:2 * k + 2, :].bitcast(F32), ALU.subtract)\
                        .then_inc(sem("merged_lo"), 1)
                through(dve, BASE[l, "O"], 4, only, loop=(l == 0))
                post_norm_dve(l, 16, ADA_TILES * l + 16)
                pre_norm_dve(l, 32, ADA_TILES * l + 24, ADA_TILES * l + 32, (H1H, H1L) if l == 0 else None)
                if l == 0:
                    states_stored(dve, 0)
                    with dve.Fori(0, 11) as i:
                        for j in range(2):
                            c = i * 2 + (GU_BASE + j)
                            lo(c + 2, None, j)
                            ada_out(c + ADA_FIRST)
                        dve.wait_ge(psum_out, i * 2 + (GU_BASE + 2))
                        dve.wait_ge(sem("ffn_lo"), i)
                        V.tensor_tensor(T2[:, :, :], T1[:, 0], T1[:, 1], ALU.mult).then_inc(sem("ffn_prod"), 1)
                        dve.wait_ge(sem("ffn_hi"), i + 1)
                        V.tensor_tensor(PRL[:, bass.ds(i * 2, 2), :], T2[:, :, :],
                                        PRH[:, bass.ds(i * 2, 2), :].bitcast(F32), ALU.subtract)\
                            .then_inc(sem("ffn_lo"), 1)
                    with dve.Fori(0, 7) as i:
                        for j in range(2):
                            c = i * 2 + (DOWN_BASE + j)
                            lo(c + 2, None, j)
                            ada_out(c + ADA_FIRST)
                    for j in range(2):
                        lo(CHUNKS - 44 + j, None, j)
                    post_norm_dve(l, 48, ADA_TILES * l + 40)

            dve.wait_ge(sem("wr_in"), 32)
            st(V.memset(LG[:, :, :], 0.0))
            b = aux()
            V.tensor_tensor(LG[:, 0:2, :], PS[:, b, 0:16].rearrange("p (t e) -> p t e", e=8),
                            BR[:, :].unsqueeze(1).broadcast_to([P, 2, NE]), ALU.add)
            V.tensor_tensor(LG[0:TS, 2, :], PS[0:TS, b, 16:24], BR[0:TS, :], ALU.add).then_inc(aux_out, 1)
            dve.wait_ge(aux_out, x[0])
            for t in range(TT):
                ins = V.max(TOPV[:, t, :], LG[:, t, :])
            st(ins)
            for t in range(TT):
                ins = V.max_index(TOPI[:, t, :], TOPV[:, t, :], LG[:, t, :])
            st(ins)
            st(V.tensor_copy(TOPF[:, :, :], TOPI[:, :, 0:2]))
            V.tensor_tensor(PR[:, :, 0:1], TOPV[:, :, 1:2], TOPV[:, :, 0:1], ALU.subtract).then_inc(sem("top_made"), 1)
            io = CF[:, C_IOTA8:C_IOTA8 + 8].unsqueeze(1).broadcast_to([P, TT, NE])
            V.tensor_tensor(S1[:, :, :], io, TOPF[:, :, 0:1].broadcast_to([P, TT, NE]), ALU.is_equal)
            st(V.tensor_tensor(S2[:, :, :], io, TOPF[:, :, 1:2].broadcast_to([P, TT, NE]), ALU.is_equal))
            st(V.tensor_tensor(SEL[:, :, :], S1[:, :, :], S2[:, :, :], ALU.add))
            see.step(V.memset(SEL[TS:P, 2, :], 0.0), sem("sel_made"))
            see.next(sem("top_exp"))
            st(V.tensor_scalar(PR[:, :, 1:2], PR[:, :, 0:1], 1.0, None, ALU.add))
            st(V.reciprocal(PR[:, :, 2:3], PR[:, :, 1:2]))
            st(V.tensor_tensor(PR[:, :, 3:4], PR[:, :, 0:1], PR[:, :, 2:3], ALU.mult))
            V.tensor_tensor(S1[:, :, :], S1[:, :, :], PR[:, :, 2:3].broadcast_to([P, TT, NE]), ALU.mult)
            st(V.tensor_tensor(S2[:, :, :], S2[:, :, :], PR[:, :, 3:4].broadcast_to([P, TT, NE]), ALU.mult))
            st(V.tensor_tensor(WT[:, :, :], S1[:, :, :], S2[:, :, :], ALU.add))
            b = aux()
            posv = PS[:, b, 0:32].rearrange("p (t e) -> p t e", e=8)
            V.tensor_copy(POS[:, :, :], posv[:, 0:TT, :])
            V.tensor_copy(CNT[:, 0, :], posv[:, 3, :]).then_inc(aux_out, 1)
            dve.wait_ge(aux_out, x[0])
            st(V.tensor_scalar(POS[:, :, :], POS[:, :, :], 1e6, None, ALU.add))
            st(V.tensor_tensor(POS[:, :, :], POS[:, :, :], SEL[:, :, :], ALU.mult))
            st(V.tensor_scalar(POS[:, :, :], POS[:, :, :], -1e6, None, ALU.add))
            V.tensor_copy(POSJ[:, :, 0:NE], POS[:, :, :])
            V.tensor_copy(WJ[:, :, 0:NE], WT[:, :, :])
            V.memset(POSJ[:, :, JOBS:], -1.0)
            V.memset(WJ[:, :, JOBS:], 0.0)
            V.tensor_scalar(CNT[:, 1, :], CNT[:, 0, :], float(P), None, ALU.is_gt)
            st(V.tensor_scalar(CNT[:, 2, :], CNT[:, 0, :], float(2 * P), None, ALU.is_gt))
            st(V.tensor_tensor(CNT[:, 3, :], CNT[:, 1, :], CNT[:, 2, :], ALU.add))
            st(V.memset(CNT[:, 4, 0:1], 0.0))
            for e in range(1, NE):
                st(V.tensor_tensor(CNT[:, 4, e:e + 1], CNT[:, 4, e - 1:e], CNT[:, 3, e - 1:e], ALU.add))
            st(V.tensor_tensor(CNT[:, 5, :], CNT[:, 4, :], CNT[:, 3, :], ALU.add))
            for k in range(EXTRA):
                V.tensor_scalar(OH[:, 0, :], CNT[:, 4, :], float(k), None, ALU.is_le)
                st(V.tensor_scalar(OH[:, 1, :], CNT[:, 5, :], float(k), None, ALU.is_gt))
                st(V.tensor_tensor(OH[:, 0, :], OH[:, 0, :], OH[:, 1, :], ALU.mult))
                st(V.tensor_scalar(OH[:, 1, :], CNT[:, 4, :], float(P), -float(P * (1 + k)), ALU.mult, ALU.add))
                st(V.tensor_tensor(JT[:, :, :], POS[:, :, :], OH[:, 1:2, :].broadcast_to([P, TT, NE]), ALU.add))
                st(V.tensor_scalar(JT[:, :, :], JT[:, :, :], 1.0, None, ALU.add))
                st(V.tensor_tensor(JT[:, :, :], JT[:, :, :], OH[:, 0:1, :].broadcast_to([P, TT, NE]), ALU.mult))
                st(V.tensor_reduce(POSJ[:, :, NE + k], JT[:, :, :], AX.X, ALU.add))
                st(V.tensor_scalar(POSJ[:, :, NE + k], POSJ[:, :, NE + k], -1.0, None, ALU.add))
                st(V.tensor_tensor(JT[:, :, :], WT[:, :, :], OH[:, 0:1, :].broadcast_to([P, TT, NE]), ALU.mult))
                st(V.tensor_reduce(WJ[:, :, NE + k], JT[:, :, :], AX.X, ALU.add))
                st(V.tensor_tensor(OH[:, 2, :], OH[:, 0, :], CF[:, C_IOTA8:C_IOTA8 + 8], ALU.mult))
                st(V.tensor_reduce(XF[:, k:k + 1], OH[:, 2, :], AX.X, ALU.add))
            st(V.tensor_copy(XF[:, 4:5], CNT[:, 5, NE - 1:NE]))
            V.tensor_copy(XI[0:1, 0:5], XF[0:1, 0:5]).then_inc(sem("routed"), 1)
            see.next(sem("routed"))
            mark["hm"] = x[0]
            for k in range(6):
                b = aux()
                dst, src = hm_unit(HML, k, x[0] - 1)
                see.next(sem("hm_hi"))
                V.tensor_tensor(dst, src, hm_unit(HMH, k, 0)[0].bitcast(F32), ALU.subtract).then_inc(aux_out, 1)
                dve.wait_ge(aux_out, x[0])
            st(V.memset(SA[:, :, :], 0.0))

            st(V.memset(YE[:, :], 0.0))
            see.step(V.memset(PTS[:, :], 0.0), y_made)

            def choose(job):
                for t in range(TT):
                    ins = V.tensor_scalar(PM[:, t, :], CF[:, C_IOTA:C_IOTA + P], POSJ[:, t, bass.ds(job, 1)], None,
                                          ALU.is_equal)
                ins.then_inc(p_made, 1)

            def choose_weighted(job):
                for t in range(TT):
                    ins = V.tensor_scalar(PW[:, t, :], CF[:, C_IOTA:C_IOTA + P], POSJ[:, t, bass.ds(job, 1)],
                                          WJ[:, t, bass.ds(job, 1)], ALU.is_equal, ALU.mult)
                ins.then_inc(sem("pw_made"), 1)

            states_stored(dve, 1)

            def m_lo_part(job, n):
                dve.wait_ge(m_hi, job * JCH + (n + 1))
                if not (isinstance(job, int) and n < 2):
                    dve.wait_ge(m_lo, job * JCH + (n - 1))
                V.tensor_tensor(MLO[:, (n - 2) % LO_RING, :], MRAW[:, n % LO_RING, :],
                                MHI[:, n % HI_RING, :].bitcast(F32), ALU.subtract).then_inc(m_lo, 1)

            def gathered(k, number):
                dve.wait_ge(m_aux_in, number + 1)
                V.tensor_copy((XEH, XEL)[k // 2][:, 4 * (k % 2):4 * (k % 2) + 4, :],
                              PS[:, 4 + k % 2, :].rearrange("p (k n) -> p k n", k=4)).then_inc(m_aux_out, 1)

            choose(0)
            for k in range(4):
                gathered(k, k)
            for n in range(HI_RING):
                m_lo_part(0, n)

            def job_dve(job):
                for c in range(JCH):
                    n = c // 2
                    if c % 2 and c < 2 * PRODS and n % 2:
                        dve.wait_ge(gate_out, job * 11 + (n // 2 + 1))
                        dve.wait_ge(m_used, job * JCH + (c + 1))
                        g = SG[:, (n // 2) * CW:(n // 2 + 1) * CW]
                        V.tensor_tensor(g, g, PS[:, n % 4, 0:CW], ALU.mult).then_inc(prod_made, 1)
                    m_lo_part(job, c + HI_RING)
                    for s, what, k in SIDE[c]:
                        bank = 4 + s % 2
                        if what == "combine":
                            dve.wait_ge(m_aux_in, job * JAUX + (AHEAD + s + 1))
                            V.tensor_tensor(SA[:, k, :], SA[:, k, :], PS[:, bank, 0:T], ALU.add)\
                                .then_inc(m_aux_out, 1)
                        elif what == "turn":
                            dve.wait_ge(gt_hi, job * 11 + (k + 1))
                            V.tensor_tensor(GTL[:, 2 * k:2 * k + 2, :],
                                            PS[:, bank, 0:2 * P].rearrange("p (k n) -> p k n", k=2),
                                            GTH[:, 2 * k:2 * k + 2, :].bitcast(F32), ALU.subtract)\
                                .then_inc(m_aux_out, 1)
                        elif what == "place":
                            dve.wait_ge(m_aux_in, job * JAUX + (AHEAD + s + 1))
                            V.tensor_copy(PTS[:, :], PS[:, bank, 0:T]).then_inc(m_aux_out, 1)
                        else:
                            dve.wait_ge(m_aux_in, job * JAUX + (AHEAD + s + 1))
                            V.tensor_copy((XEH, XEL)[k // 2][:, 4 * (k % 2):4 * (k % 2) + 4, :],
                                          PS[:, bank, :].rearrange("p (k n) -> p k n", k=4)).then_inc(m_aux_out, 1)
                    if c == 2 * KD + 2:
                        choose_weighted(job)
                        choose(job + 1)

            with dve.Fori(0, NE) as job:
                dve.wait_ge(m_aux_out, job * JAUX + AHEAD)
                job_dve(job)
            dve.wait_ge(sem("routed"), 1)
            extra = dve.value_load(XI[0:1, 4:5], min_val=0, max_val=EXTRA)
            with dve.Fori(0, EXTRA) as k:
                with dve.If(k < extra):
                    dve.wait_ge(m_aux_out, k * JAUX + (NE * JAUX + AHEAD))
                    job_dve(k + NE)
            dve.wait_ge(m_aux_out, extra * JAUX + (NE * JAUX + AHEAD))
            for d in range(KD):
                dve.wait_ge(m_aux_in, extra * JAUX + (NE * JAUX + AHEAD + d + 1))
                V.tensor_tensor(SA[:, d, :], SA[:, d, :], PS[:, 4 + d % 2, 0:T], ALU.add).then_inc(m_aux_out, 1)
            dve.wait_ge(m_aux_out, extra * JAUX + (NE * JAUX + AHEAD + KD))
            post_norm_dve(1, 48, ADA_TILES + 40)
            for k in range(6):
                b = aux()
                t, h = k // 2, k % 2
                n = P if t < 2 else TS
                ins = V.tensor_copy(XTM[0:n, t, 512 * h:512 * h + 512], PS[0:n, b, :])
                ins.then_inc(aux_out, 1)
            mark["y"] = x[0]

        @block.scalar
        def _(act):
            see = Seen(act)
            A = nc.scalar

            def hi(c, r, j):
                if isinstance(c, int) and c >= CHUNKS:
                    return
                act.wait_ge(raw_in[j], r * 16 + 16)
                if not (isinstance(c, int) and c < 2):
                    act.wait_ge(chunk_used, c - 1)
                A.activation(WHI[:, j, :], RAW[:, j, :], ACT.Copy).then_inc(hi_made, 1)

            nsq = [0]

            def square(src):
                if nsq[0] >= 4:
                    act.wait_ge(sq_used, nsq[0] - 3)
                A.activation(square_slot(nsq[0]), src, ACT.Square).then_inc(sq_made, 1)
                nsq[0] += 1

            def root(n):
                see.next(ms_made)
                A.activation(RST[:, 0:n], RST[:, 0:n], ACT.Sqrt).then_inc(std_made, 1)

            def square_x(number):
                for d in range(KD):
                    if number:
                        act.wait_ge(x_ready, KD * (number - 1) + d + 1)
                    square(X[:, d, :])
                root(T)

            def pre_norm_act(l, sh, parts):
                see.next(sem("hs_made"))
                if parts is not None:
                    A.activation(v3(parts)[:, :, TP:T], HT[:, :, TP:T], ACT.Copy).then_inc(sem("h_hi"), 1)
                for d in range(KD):
                    see.next(sem("xr_made"))
                    if parts is None:
                        A.activation(HT[:, d, 0:TP], HT[:, d, 0:TP], ACT.Identity, bias=MOD[:, sh + d, 0:1])\
                            .then_inc(sem("hp_made"), 1)
                    else:
                        A.activation(v3(parts)[:, d, 0:TP], HT[:, d, 0:TP], ACT.Identity, bias=MOD[:, sh + d, 0:1])\
                            .then_inc(sem("h_hi"), 1)

            def v3(t):
                return t[:, 0:KD * T].rearrange("p (k t) -> p k t", k=KD)

            act.dma_start(CT[0:1, :], a["c_prompt"]).then_inc(sem("c_in"), 16)
            act.dma_start(CT[1:SEQS, :], a["c_sample"]).then_inc(sem("c_in"), 16)
            xtm = sem("xtm_in")
            act.dma_start(XTM[:, 0:2, :], a["x_prompt"][0].rearrange("(t p) d -> p t d", p=P)).then_inc(xtm, 16)
            act.dma_start(XTM[0:TS, 2, :], a["x_sample"].rearrange("s t d -> (s t) d")).then_inc(xtm, 16)
            act.wait_ge(sem("c_in"), 32)
            A.activation(CT[:, :], CT[:, :], ACT.Silu).then_inc(sem("c_made"), 1)
            see.next(sem("lb_shifted"))
            A.activation(LT[:, 0:2, :], LT[:, 0:2, :], ACT.Exp).then_inc(sem("lb_exp"), 1)
            act.wait_ge(aux_out, 5)
            square_x(0)
            for c in range(2):
                act.wait_ge(ada_used, 10 + 2 * c)
                hi(c, 0, c)
            for l in range(DEPTH):
                pre_norm_act(l, ADA_TILES * l, H1H)

                def banks(j):
                    return PS[:, 2 * j:2 * j + 2, 0:T]

                def plain(dst, func, scale=1.0):
                    def one(c, r, j, n):
                        act.wait_ge(chunk_used, c + 1)
                        A.activation(dst[:, bass.ds(n * 2, 2), :], banks(j), func, scale=scale).then_inc(psum_out, 1)
                        hi(c + 2, r + 1, j)
                    return one

                def gates(c, r, j, n):
                    act.wait_ge(chunk_used, c + 1)
                    A.activation(KK[:, bass.ds(n * 2, 2), :], banks(j), ACT.Sigmoid, scale=-1.0)
                    A.activation(FG[:, bass.ds(n * 2, 2), :], banks(j), ACT.Sigmoid).then_inc(psum_out, 1)
                    hi(c + 2, r + 1, j)

                def token_major(dst, func):
                    def one(c, r, j, n):
                        act.wait_ge(chunk_used, c + 1)
                        A.activation(dst[:, 0:2, bass.ds(n * CW, CW)],
                                     PS[:, 2 * j, :].rearrange("p (t n) -> p t n", t=2), func)
                        A.activation(dst[0:TS, 2, bass.ds(n * CW, CW)], PS[0:TS, 2 * j + 1, 0:CW],
                                     func).then_inc(psum_out, 1)
                        hi(c + 2, r + 1, j)
                    return one

                through(act, BASE[l, "f"], 4, gates)
                through(act, BASE[l, "q"], 4, plain(QQ, ACT.Silu))
                through(act, BASE[l, "i"], 4, token_major(IT, ACT.Copy))
                through(act, BASE[l, "v"], 4, token_major(VT, ACT.Gelu), loop=False)
                see.next(sem("var_made"))
                A.activation(MV[:, :, 2:3], MV[:, :, 2:3], ACT.Sqrt).then_inc(sem("vstd_made"), 1)

                for k in range(4):
                    c, j = BASE[l, "u"] + k, k % 2
                    act.wait_ge(chunk_used, c + 1)
                    if k or l:
                        act.wait_ge(sem("a_made"), 4 * l + k)
                    A.activation(T1[:, 0], banks(j), ACT.Gelu).then_inc(psum_out, 1)
                    hi(c + 2, (c + 2) // 2, j)
                    act.wait_ge(sem("a_made"), 4 * l + k + 1)
                    A.activation(v3(H2H)[:, 2 * k:2 * k + 2, :], T2[:, :, :], ACT.Copy).then_inc(sem("a_hi"), 1)
                act.wait_ge(sem("v_stored"), 16 * (l + 1))
                act.wait_ge(sem("mixed"), 4 * l + 4)
                through(act, BASE[l, "g"], 4, plain(GS, ACT.Silu), loop=False)
                act.wait_ge(sem("level_made"), 8 * l + 8)
                through(act, BASE[l, "A"], 4, plain(SA, ACT.Copy), loop=False)

                def o_square():
                    A.activation(OSQ[:, :], OT[:, :], ACT.Square).then_inc(sq_made, 1)
                    nsq[0] += 1

                for k in range(4):
                    c, j = BASE[l, "ga"] + k, k % 2
                    act.wait_ge(chunk_used, c + 1)
                    act.wait_ge(sem("ga_used"), 4 * l + k)
                    A.activation(T1[:, 1], banks(j), ACT.Sigmoid).then_inc(psum_out, 1)
                    hi(c + 2, (c + 2) // 2, j)
                    if k:
                        root(512)
                    act.wait_ge(aux_out, mark["o", l, k])
                    o_square()

                def alone(s):
                    if s >= 2:
                        act.wait_ge(aux_out, mark["st", l, s - 2])
                    A.activation(IM[:, s % 2, :], IT[0:TS, 2, :], ACT.Copy,
                                 scale=CF[0:TS, C_SEQ + s:C_SEQ + s + 1]).then_inc(sem("im_made"), 1)

                alone(0)
                alone(1)
                for k in range(4):
                    c, j = BASE[l, "gb"] + k, k % 2
                    act.wait_ge(chunk_used, c + 1)
                    A.activation(GB[:, 2 * k:2 * k + 2, :], banks(j), ACT.Sigmoid).then_inc(psum_out, 1)
                    if k == 0:
                        root(512)
                    hi(c + 2, (c + 2) // 2, j)
                    if k < 3:
                        alone(2 * k + 2)
                        alone(2 * k + 3)
                for d in range(0, KD, 2):
                    A.activation(v3(H1H)[:, d:d + 2, 0:TP], HT[:, d:d + 2, 0:TP], ACT.Copy).then_inc(sem("h_hi"), 1)
                see.next(sem("os_out"))
                o_square()
                root(512)
                act.wait_ge(sem("on_made"), 5 * l + 5)
                A.activation(v3(H1H)[:, :, TP:T], HT[:, :, TP:T], ACT.Copy).then_inc(sem("h_hi"), 1)
                for n in range(2):
                    act.wait_ge(sem(f"st_stored{n}"), 16 * 2 * (l + 1))
                for k in range(4):
                    c, j = BASE[l, "B"] + k, k % 2
                    act.wait_ge(chunk_used, c + 1)
                    act.wait_ge(sem("merged"), 4 * l + k)
                    A.activation(T1[:, 0], banks(j), ACT.Copy).then_inc(psum_out, 1)
                    hi(c + 2, (c + 2) // 2, j)
                    act.wait_ge(sem("merged"), 4 * l + k + 1)
                    A.activation(v3(H2H)[:, 2 * k:2 * k + 2, :], SA[:, 2 * k:2 * k + 2, :],
                                 ACT.Copy).then_inc(sem("merged_hi"), 1)
                for k in range(4):
                    c = BASE[l, "O"] + k
                    plain(SA, ACT.Copy)(c, c // 2, k % 2, k)
                    act.wait_ge(psum_out, c + 1)
                    for m in range(2):
                        square(SA[:, 2 * k + m, :])
                root(T)
                square_x(2 * l + 1)
                pre_norm_act(l, ADA_TILES * l + 24, H1H if l == 0 else None)
                if l == 0:
                    states_stored(act, 0)
                    with act.Fori(0, 11) as i:
                        for j in range(2):
                            c = i * 2 + (GU_BASE + j)
                            act.wait_ge(chunk_used, c + 1)
                            act.wait_ge(sem("ffn_prod"), i)
                            A.activation(T1[:, j], banks(j), (ACT.Silu, ACT.Copy)[j]).then_inc(psum_out, 1)
                            hi(c + 2, i + (GU_BASE // 2 + 1), j)
                        act.wait_ge(sem("ffn_prod"), i + 1)
                        A.activation(PRH[:, bass.ds(i * 2, 2), :], T2[:, :, :], ACT.Copy).then_inc(sem("ffn_hi"), 1)
                    with act.Fori(0, 4) as i:
                        for u in range(2):
                            c = i * 4 + (DOWN_BASE + 2 * u)
                            r = i * 2 + (DOWN_BASE // 2 + u)
                            act.wait_ge(chunk_used, c + 1)
                            hi(c + 2, r + 1, 0)
                            act.wait_ge(chunk_used, c + 2)
                            A.activation(SA[:, bass.ds(i * 2 + u, 1), :], PS[:, 2 * u:2 * u + 1, 0:T],
                                         ACT.Copy).then_inc(psum_out, 2)
                            hi(c + 3, r + 1, 1)
                            act.wait_ge(sq_used, i * 2 + (nsq[0] + u - 1))
                            A.activation(square_slot(nsq[0] + u), PS[:, 2 * u, 0:T], ACT.Square).then_inc(sq_made, 1)
                    nsq[0] += KD
                    root(T)
                    square_x(2)

            see.next(sem("top_made"))
            A.activation(PR[:, :, 0:1], PR[:, :, 0:1], ACT.Exp).then_inc(sem("top_exp"), 1)
            for k in range(6):
                act.wait_ge(aux_in, mark["hm"] + k + 1)
                A.activation(*hm_unit(HMH, k, mark["hm"] + k), ACT.Copy).then_inc(sem("hm_hi"), 1)
            states_stored(act, 1)

            def m_hi_part(job, n):
                act.wait_ge(m_raw[n % LO_RING], job * (16 * (JCH // LO_RING)) + 16 * (n // LO_RING + 1))
                if n >= HI_RING:
                    act.wait_ge(m_used, job * JCH + (n - HI_RING + 1))
                A.activation(MHI[:, n % HI_RING, :], MRAW[:, n % LO_RING, :], ACT.Copy).then_inc(m_hi, 1)

            for n in range(HI_RING):
                m_hi_part(0, n)

            def job_act(job):
                for c in range(JCH):
                    n = c // 2
                    if c % 2 and c < 2 * PRODS and n % 2 == 0:
                        act.wait_ge(m_used, job * JCH + (c + 1))
                        A.activation(SG[:, (n // 2) * CW:(n // 2 + 1) * CW], PS[:, n % 4, 0:CW],
                                     ACT.Silu).then_inc(gate_out, 1)
                    if c == JCH - 1:
                        act.wait_ge(m_used, job * JCH + JCH)
                        A.activation(YE[:, :].rearrange("p (k n) -> p k n", k=2), PS[:, 6:8, :],
                                     ACT.Copy).then_inc(y_made, 1)
                    m_hi_part(job, c + HI_RING)
                    for s, what, k in SIDE[c]:
                        if what == "turn":
                            act.wait_ge(m_aux_in, job * JAUX + (AHEAD + s + 1))
                            A.activation(GTH[:, 2 * k:2 * k + 2, :],
                                         PS[:, 4 + s % 2, 0:2 * P].rearrange("p (k n) -> p k n", k=2), ACT.Copy)\
                                .then_inc(gt_hi, 1)

            with act.Fori(0, NE) as job:
                job_act(job)
            act.wait_ge(sem("routed"), 1)
            extra = act.value_load(XI[0:1, 4:5], min_val=0, max_val=EXTRA)
            with act.Fori(0, EXTRA) as k:
                with act.If(k < extra):
                    job_act(k + NE)
            for d in range(KD):
                act.wait_ge(m_aux_out, extra * JAUX + (NE * JAUX + AHEAD + d + 1))
                square(SA[:, d, :])
            root(T)

        @block.gpsimd
        def _(pool):
            see = Seen(pool)
            small = sem("small_in")
            pool.dma_start(CF[:, :], a["const_f"]).then_inc(small, 16)
            pool.dma_start(SC[:, 0:8 * P].rearrange("p (l t) -> p l t", l=8), a["const_m"]).then_inc(sem("mask_in"), 16)
            vec = sem("vec_in")
            pool.dma_start(VR[0:96, 0, :], a["b_ada"].rearrange("l (j p) -> (l j) p", p=P)).then_inc(vec, 16)
            for n, k in enumerate(("norm_pre_mix", "norm_post_mix", "norm_pre_ffn", "norm_post_ffn", "hg_lb_raw")):
                pool.dma_start(VR[16 * n:16 * n + 16, 1, :],
                               a[k].rearrange("l (j p) -> (l j) p", p=P)).then_inc(vec, 16)
            pool.dma_start(VR[80:82, 1, :], a["hg_norm_w"]).then_inc(vec, 16)
            pool.memset(ONES[:, :], 1.0).then_inc(sem("ones_set"), 1)
            for t in (H1H, H1L):
                pool.memset(t[:, KD * T:KD * T + 64].bitcast(F32), 0.0).then_inc(sem("tail_set"), 1)

            pool.wait_ge(sem("mask_in"), 16)
            pool.tensor_copy(CM[:, :, :], SC[:, 0:8 * P].rearrange("p (l t) -> p l t", l=8)).then_inc(sem("mask_made"), 1)
            see.next(sem("mask_made"))

            for l in range(DEPTH):
                if l:
                    pool.wait_ge(chunk_used, GU_BASE)
                ws_in, bs_in = sem("ws_in"), sem("bs_in")
                pool.memset(WSRS[:, :, :], 0.0).then_inc(sem("wsrs_zero"), 1)
                pool.dma_start(LNW[:, :], a["gm_ln_w"][l:l + 1, :].broadcast_to([P, D])).then_inc(sem("ln_in"), 16)
                pool.dma_start(LNB[:, :], a["gm_ln_b"][l:l + 1, :].broadcast_to([P, D])).then_inc(sem("ln_in"), 16)
                pool.dma_start(WSR[:, :, :], a["gm_ws"][l].rearrange("g t s -> t g s")).then_inc(ws_in, 16)
                see.next(sem("wsrs_zero"))
                for s in range(NS):
                    pool.dma_start(WSRS[s * LS:(s + 1) * LS, :, s * LS:(s + 1) * LS],
                                   a["gm_ws"][l, :, 0:LS, 0:LS].rearrange("g t s -> t g s")).then_inc(ws_in, 16)
                if l:
                    pool.wait_ge(x_ready, 2 * KD)
                for g in range(G4):
                    row = a["gm_bs"][l, g:g + 1, :]
                    for t in range(2):
                        pool.dma_start(BGS[32 * g:32 * g + 1, t * P:(t + 1) * P], row).then_inc(bs_in, 16)
                    pool.dma_start(BGS[32 * g:32 * g + 1, TP:T].rearrange("p (s t) -> p s t", s=NS),
                                   row[:, 0:LS].unsqueeze(1).broadcast_to([1, NS, LS])).then_inc(bs_in, 16)
                pool.memset(SC[:, :], 0.0).then_inc(sem("sc_zero"), 1)
                see.next(sem("v_ready"))
                pool.dma_start(out["v"][l].rearrange("s t d -> (s t) d"), VT[0:TS, 2, :]).then_inc(sem("v_stored"), 16)
                def load_state(s):
                    t, place = state(s)
                    if s < 2:
                        pool.wait_ge(chunk_used, BASE[l, "A"] + 4)
                    elif s == 2:
                        pool.wait_ge(aux_out, mark["o", l, 3])
                    elif s == 3:
                        pool.wait_ge(sem("sp_stored"), 16 * (l + 1))
                    else:
                        pool.wait_ge(sem(f"st_stored{place}"), 16 * (2 * l + 1))
                    pool.dma_start(t, a["state_hgrn"][l, s].rearrange("h k v -> k h v"))\
                        .then_inc(sem(f"st_in{place}"), 16)

                pool.wait_ge(aux_out, mark["s2", l])
                pool.dma_start(out["sp"][l, 0].rearrange("h k v -> k h v"), ST[:, 1]).then_inc(sem("sp_stored"), 16)
                for s in range(3):
                    load_state(s)
                for s in range(NS):
                    if s + 3 < NS:
                        load_state(s + 3)
                    t, place = state(s)
                    pool.wait_ge(aux_out, mark["st", l, s])
                    pool.dma_start(out["ss"][l, s].rearrange("h k v -> k h v"), t)\
                        .then_inc(sem(f"st_stored{place}"), 16)
            pool.wait_ge(chunk_used, CHUNKS)
            pool.dma_start(WR[:, :, :], a["w_router"][0].rearrange("(k p) e -> p k e", p=P)).then_inc(sem("wr_in"), 16)
            pool.dma_start(BR[:, :], a["b_router"][0:1, :].broadcast_to([P, NE])).then_inc(sem("wr_in"), 16)
            pool.wait_ge(aux_out, mark["y"])
            pool.dma_start(out["yp"][0].rearrange("(t p) d -> p t d", p=P), XTM[:, 0:2, :]).then_inc(sem("y_stored"), 16)
            pool.dma_start(out["ys"].rearrange("s t d -> (s t) d"), XTM[0:TS, 2, :]).then_inc(sem("y_stored"), 16)
            pool.wait_ge(sem("v_stored"), 32)
            states_stored(pool, 1)
            pool.wait_ge(sem("y_stored"), 32)

        @block.tensor
        def _(pe):
            M = nc.tensor
            x = [0]
            counts = {"norms": 0, "sq": 0}

            def aux():
                if x[0] >= 2:
                    pe.wait_ge(aux_out, x[0] - 1)
                x[0] += 1
                return 4 + (x[0] - 1) % 2

            def stat(first, last, n=T, src=None):
                if first:
                    if counts["norms"]:
                        pe.wait_ge(ms_made, counts["norms"])
                    counts["norms"] += 1
                counts["sq"] += 1
                pe.wait_ge(sq_made, counts["sq"])
                M.matmul(PS[:, 6, 0:n], ONES[:, :], square_slot(counts["sq"] - 1) if src is None else src,
                         start=first, stop=last).then_inc(sq_used, 1)

            def stats(tiles=range(KD)):
                for k in tiles:
                    stat(k == 0, k == KD - 1)

            def ada_product(t, w):
                if not (isinstance(t, int) and t == 0):
                    pe.wait_ge(ada_made, t)
                for k in range(KD):
                    ins = M.matmul(PS[:, 7, 0:SEQS], w[:, k, :], CS[:, k, :], start=(k == 0), stop=(k == KD - 1))
                ins.then_inc(ada_used, 1)

            def ada(c, r, j):
                pe.wait_ge(ada_in[j], r * 16 + 16)
                ada_product(c + ADA_FIRST, ADA[:, j])

            def three(out_, w, v, start, stop):
                M.matmul(out_, w[0], v[0], start=start, stop=False)
                M.matmul(out_, w[0], v[1], start=False, stop=False)
                return M.matmul(out_, w[1], v[0], start=False, stop=stop)

            def chunk_start(c):
                pe.wait_ge(lo_made, c + 1)
                if not (isinstance(c, int) and c < 2):
                    pe.wait_ge(psum_out, c - 1)

            def channels(parts, l, ready=None):
                def one(c, r, j, n):
                    chunk_start(c)
                    for m in range(2):
                        for k in range(KD):
                            s = slice(k * CW + m * P, k * CW + (m + 1) * P)
                            t = slice(k * T, (k + 1) * T)
                            if ready is not None and m == 0:
                                pe.wait_ge(operand, ready + k + 1)
                            ins = three(PS[:, 2 * j + m, 0:T], (WHI[:, j, s], WLO[:, j, s]),
                                        (parts[0][:, t], parts[1][:, t]), k == 0, k == KD - 1)
                    ins.then_inc(chunk_used, 1)
                    if l == 0:
                        ada(c, r, j)
                return one

            def tokens(parts, l):
                def one(c, r, j, n):
                    chunk_start(c)
                    for t in range(TT):
                        o_ = PS[:, 2 * j + t // 2, CW * (t % 2):CW * (t % 2) + CW]
                        for k in range(KD):
                            s = slice(k * CW, (k + 1) * CW)
                            q = slice(k * T + t * P, k * T + (t + 1) * P)
                            ins = three(o_, (parts[0][:, q], parts[1][:, q]), (WHI[:, j, s], WLO[:, j, s]),
                                        k == 0, k == KD - 1)
                    ins.then_inc(chunk_used, 1)
                    if l == 0:
                        ada(c, r, j)
                return one

            H1, H2 = (H1H, H1L), (H2H, H2L)

            pe.wait_ge(sem("small_in"), 16)
            pe.wait_ge(sem("xtm_in"), 32)
            for k in range(5):
                b = aux()
                if k < 4:
                    for d in range(4):
                        kd = 4 * (k % 2) + d
                        ins = M.transpose(PS[:, b, d * P:(d + 1) * P], XTM[:, k // 2, kd * P:(kd + 1) * P], ident)
                else:
                    for d in range(KD):
                        ins = M.transpose(PS[:, b, d * TS:(d + 1) * TS], XTM[0:TS, 2, d * P:(d + 1) * P],
                                          CF[0:TS, C_ID:C_ID + TS])
                ins.then_inc(aux_in, 1)
            pe.wait_ge(sem("vec_in"), 16 * 7)
            b = aux()
            M.transpose(PS[:, b, 0:96], VR[0:96, 0, :], CF[0:96, C_ID:C_ID + 96])
            M.transpose(PS[:, b, P:P + 82], VR[0:82, 1, :], CF[0:82, C_ID:C_ID + 82]).then_inc(aux_in, 1)
            pe.wait_ge(sem("c_made"), 1)
            b = aux()
            for d in range(KD):
                ins = M.transpose(PS[:, b, d * 16:d * 16 + SEQS], CT[:, d * P:(d + 1) * P], CF[0:SEQS, C_ID:C_ID + SEQS])
            ins.then_inc(aux_in, 1)
            pe.wait_ge(sem("ones_set"), 1)
            pe.wait_ge(aux_out, 7)
            stats()
            for t in range(ADA_FIRST):
                n = t // 2
                pe.wait_ge(sem(f"first_in{n % 4}"), 16 * (n // 4 + 1))
                ada_product(t, first_ada(n)[:, :, P * (t % 2):P * (t % 2) + P])

            n_operand = 0
            for l in range(DEPTH):
                if l == 0:
                    pe.wait_ge(sem("tail_set"), 2)
                for k in range(4):
                    c = BASE[l, "f"] + k
                    channels(H1, l, n_operand if k == 0 else None)(c, c // 2, k % 2, k)
                n_operand += KD
                through(pe, BASE[l, "q"], 4, channels(H1, l))
                through(pe, BASE[l, "i"], 4, tokens(H1, l))

                def scores(units):
                    for k in range(units):
                        b = aux()
                        for h in range(4 if k < 4 else 8):
                            if k < 4:
                                hh, t0, n = 4 * (k % 2) + h, P * (k // 2), P
                            else:
                                hh, t0, n = h, TP, TS
                            ins = M.matmul(PS[0:n, b, h * n:(h + 1) * n], KK[:, hh, t0:t0 + n], QQ[:, hh, t0:t0 + n],
                                           start=True, stop=True)
                        ins.then_inc(aux_in, 1)

                def level(n):
                    pe.wait_ge(sem("level_made"), 8 * l + n + 1)
                    scores(5 if LEVELS[n] < LS else 4)

                for k in range(4):
                    c = BASE[l, "v"] + k
                    tokens(H1, l)(c, c // 2, k % 2, k)
                    if k == 0:
                        pe.wait_ge(sem("k_ready"), l + 1)
                        pe.wait_ge(psum_out, BASE[l, "i"] + 4)
                        scores(5)
                    else:
                        level(k - 1)
                pe.wait_ge(sem("ws_in"), 16 * 9 * (l + 1))
                b = aux()
                for g in range(G4):
                    ins = M.transpose(PS[:, b, g * P:(g + 1) * P], WSR[:, g, :], ident)
                ins.then_inc(aux_in, 1)
                b = aux()
                for g in range(G4):
                    ins = M.transpose(PS[0:TS, b, g * TS:(g + 1) * TS], WSRS[:, g, :], CF[0:TS, C_ID:C_ID + TS])
                ins.then_inc(aux_in, 1)
                for k in range(4):
                    c = BASE[l, "u"] + k
                    channels(H1, l)(c, c // 2, k % 2, k)
                    if k == 0:
                        pe.wait_ge(sem("v_ready"), l + 1)
                        pe.wait_ge(sem("bs_in"), 16 * 12 * (l + 1))
                    pe.wait_ge(aux_out, x[0])
                    if k or l:
                        pe.wait_ge(sem("a_made"), 4 * l + k)
                    for m in range(2):
                        n = 2 * k + m
                        g, s = n // 2, slice(n * P, (n + 1) * P)
                        o_ = PS[:, 4 + m, :]
                        M.matmul(o_[:, 0:T], ONES[32 * g:32 * g + 1, :], BGS[32 * g:32 * g + 1, :], start=True, stop=False,
                                 skip_group_check=True)
                        M.matmul(o_[:, 0:P], VT[:, 0, s], WST[:, g, :], start=False, stop=False, skip_group_check=True)
                        M.matmul(o_[:, P:TP], VT[:, 1, s], WST[:, g, :], start=False, stop=False, skip_group_check=True)
                        ins = M.matmul(o_[:, TP:T], VT[0:TS, 2, s], WSS[:, g, :], start=False, stop=True,
                                       skip_group_check=True)
                    ins.then_inc(sem("mixed"), 1)
                    if k in (1, 3):
                        pe.wait_ge(sem("a_made"), 4 * l + k + 1)
                        level(3 + k // 2)
                for k in range(4):
                    c = BASE[l, "g"] + k
                    channels(H1, l)(c, c // 2, k % 2, k)
                    if k in (1, 3):
                        level(5 + k // 2)
                pe.wait_ge(sem("a_lo"), 4 * l + 4)
                for k in range(4):
                    c = BASE[l, "A"] + k
                    channels(H2, l)(c, c // 2, k % 2, k)
                    if k == 0:
                        pe.wait_ge(sem("level_made"), 8 * l + 8)
                        for n in range(4):
                            b = aux()
                            for h in range(4):
                                ins = M.transpose(PS[:, b, h * P:(h + 1) * P],
                                                  KK[:, 4 * (n % 2) + h, P * (n // 2):P * (n // 2) + P], ident)
                            ins.then_inc(aux_in, 1)
                        for n in range(2):
                            b = aux()
                            for h in range(4):
                                ins = M.transpose(PS[0:TS, b, h * P:(h + 1) * P], KK[:, 4 * n + h, TP:T], ident)
                            ins.then_inc(aux_in, 1)
                    if k in (1, 2):
                        pe.wait_ge(aux_out, x[0])
                        for n in range(2):
                            b = aux()
                            for h in range(4):
                                s = slice((4 * n + h) * P, (4 * n + h + 1) * P)
                                ins = M.matmul(PS[:, b, h * P:(h + 1) * P], KTM[:, k - 1, s], IT[:, k - 1, s],
                                               start=True, stop=True)
                            ins.then_inc(aux_in, 1)
                for k in range(4):
                    c = BASE[l, "ga"] + k
                    channels(H1, l)(c, c // 2, k % 2, k)
                    if k:
                        stat(True, True, 512, OSQ[:, :])
                    pe.wait_ge(aux_out, x[0])
                    b = aux()
                    for hh in range(2):
                        h = 2 * k + hh
                        s, q = slice(h * P, (h + 1) * P), (h % 4) * P
                        for t in range(2):
                            o_ = PS[:, b, hh * TP + t * P:hh * TP + (t + 1) * P]
                            u0 = (2 * t + h // 4) * 512 + q
                            ins = M.matmul(o_, IT[:, t, s], SC[:, u0:u0 + P], start=True, stop=(t == 0))
                            if t:
                                ins = M.matmul(o_, ST[:, 0, h, :], QQ[:, h, P:TP], start=False, stop=True)
                    ins.then_inc(aux_in, 1)
                for k in range(4):
                    c = BASE[l, "gb"] + k
                    channels(H1, l)(c, c // 2, k % 2, k)
                    if k == 0:
                        stat(True, True, 512, OSQ[:, :])
                        pe.wait_ge(ms_made, counts["norms"])
                        for h in range(HEADS):
                            ins = M.matmul(PS[:, 6, h * TS:(h + 1) * TS], IT[0:TS, 2, h * P:(h + 1) * P],
                                           SC[0:TS, 2048 + h * TS:2048 + (h + 1) * TS], start=(h == 0), stop=False,
                                           skip_group_check=True)
                        ins.then_inc(sem("sc_used"), 1)
                    for s in (2 * k, 2 * k + 1):
                        old, place = state(s)
                        pe.wait_ge(sem(f"st_in{place}"), 16 * (2 * l + s // 4 + 1))
                        for h in range(HEADS):
                            t0 = TP + s * LS
                            ins = M.matmul(PS[:, 6, h * TS + s * LS:h * TS + (s + 1) * LS], old[:, h, :],
                                           QQ[:, h, t0:t0 + LS], start=False, stop=(s == NS - 1 and h == HEADS - 1),
                                           skip_group_check=True)
                        ins.then_inc(sem("st_read"), 1)
                        pe.wait_ge(sem("im_made"), 8 * l + s + 1)
                        for n in range(2):
                            b = aux()
                            for h in range(4):
                                q = slice((4 * n + h) * P, (4 * n + h + 1) * P)
                                ins = M.matmul(PS[:, b, h * P:(h + 1) * P], KTM[0:TS, 2, q], IM[:, s % 2, q],
                                               start=True, stop=True)
                            ins.then_inc(aux_in, 1)
                stat(True, True, 512, OSQ[:, :])
                n_operand += 1
                pe.wait_ge(operand, n_operand)
                through(pe, BASE[l, "B"], 4, channels(H1, l), loop=False)
                pe.wait_ge(sem("merged_lo"), 4 * l + 4)
                for k in range(4):
                    c = BASE[l, "O"] + k
                    channels(H2, l)(c, c // 2, k % 2, k)
                    if k:
                        stats(range(2 * k - 2, 2 * k))
                stats(range(KD - 2, KD))
                stats()
                if l == 0:
                    for j in range(2):
                        channels(H1, l, None if j else n_operand)(GU_BASE + j, GU_BASE // 2, j, None)
                    n_operand += KD
                    with pe.Fori(1, 11) as i:
                        for j in range(2):
                            channels(H1, l)(i * 2 + (GU_BASE + j), i + GU_BASE // 2, j, None)
                    pe.wait_ge(sem("ffn_lo"), 11)

                    def down(u, c, r, with_ada):
                        for j in range(2):
                            pe.wait_ge(lo_made, c + j + 1)
                            if j == 0:
                                pe.wait_ge(psum_out, c - 1 if u is None else c)
                            for k in range(11):
                                s = slice(k * P, (k + 1) * P)
                                kf = 11 * j + k
                                bank = 2 * (0 if u is None else u)
                                ins = three(PS[:, bank, 0:T], (WHI[:, j, s], WLO[:, j, s]),
                                            (PRH[:, kf, :], PRL[:, kf, :]), kf == 0, kf == KF - 1)
                            ins.then_inc(chunk_used, 1)
                            if with_ada:
                                ada(c + j, r, j)
                    first = counts["sq"]

                    def tile(i, u, with_ada=True):
                        down(u, i * 4 + (DOWN_BASE + 2 * u), i * 2 + (DOWN_BASE // 2 + u), with_ada)

                    tile(0, 0)
                    tile(0, 1)
                    stat(True, False)
                    with pe.Fori(1, 3) as i:
                        for u in range(2):
                            tile(i, u)
                            pe.wait_ge(sq_made, i * 2 + (first + u))
                            M.matmul(PS[:, 6, 0:T], ONES[:, :], square_slot(first + 1 - u), start=False, stop=False)\
                                .then_inc(sq_used, 1)
                    counts["sq"] += 4
                    tile(3, 0)
                    stat(False, False, src=square_slot(first + 1))
                    tile(3, 1, False)
                    stat(False, False, src=square_slot(first))
                    stat(False, True, src=square_slot(first + 1))
                    stats()

            pe.wait_ge(sem("hp_made"), KD)
            pe.wait_ge(sem("hs_made"), 4)
            pe.wait_ge(sem("wr_in"), 32)
            b = aux()
            for t in range(TT):
                n = P if t < 2 else TS
                for k in range(KD):
                    ins = M.matmul(PS[0:n, b, 8 * t:8 * t + 8], HT[:, k, t * P:t * P + n], WR[:, k, :],
                                   start=(k == 0), stop=(k == KD - 1))
            ins.then_inc(aux_in, 1)
            pe.wait_ge(sem("sel_made"), 1)
            b = aux()
            for t in range(TT + 1):
                o_ = PS[:, b, 8 * t:8 * t + 8]
                for e in range(min(t, TT)):
                    ins = M.matmul(o_, ONES[:, :], SEL[:, e, :], start=(e == 0), stop=(t == TT and e == TT - 1))
                if t < TT:
                    ins = M.matmul(o_, CF[:, C_TRI:C_TRI + P], SEL[:, t, :], start=(t == 0), stop=True)
            ins.then_inc(aux_in, 1)
            for k in range(6):
                b = aux()
                n, t0 = (P if k < 4 else TS), P * (k // 2)
                for d in range(4):
                    ins = M.transpose(PS[0:n, b, d * P:(d + 1) * P], HT[:, 4 * (k % 2) + d, t0:t0 + n], ident)
                ins.then_inc(aux_in, 1)
            pe.wait_ge(aux_out, x[0])

            def gather(k, bank):
                for d in range(4):
                    s = slice((4 * (k % 2) + d) * P, (4 * (k % 2) + d + 1) * P)
                    for t in range(TT):
                        n = P if t < 2 else TS
                        ins = M.matmul(PS[:, bank, d * P:(d + 1) * P], (HMH, HML)[k // 2][0:n, t, s], PM[0:n, t, :],
                                       start=(t == 0), stop=(t == TT - 1))
                return ins

            def combine(d, bank):
                return M.matmul(PS[:, bank, 0:T], YE[:, d * P:(d + 1) * P], PTS[:, :], start=True, stop=True)

            pe.wait_ge(p_made, 1)
            for k in range(4):
                if k >= 2:
                    pe.wait_ge(m_aux_out, k - 1)
                gather(k, 4 + k % 2).then_inc(m_aux_in, 1)

            def job_pe(job):
                pe.wait_ge(m_aux_out, job * JAUX + AHEAD)
                for c in range(JCH):
                    pe.wait_ge(m_lo, job * JCH + (c + 1))
                    hi_, lo_ = MHI[:, c % HI_RING, :], MLO[:, (c - 2) % LO_RING, :]
                    if c < 2 * PRODS:
                        n = c // 2
                        if c % 2 == 0 and n >= 2:
                            pe.wait_ge((gate_out, prod_made)[n % 2], job * 11 + (n // 2 - 1))
                        for q in range(4):
                            k, s = 4 * (c % 2) + q, slice(q * CW, (q + 1) * CW)
                            ins = three(PS[:, n % 4, 0:CW], (XEH[:, k, :], XEL[:, k, :]), (hi_[:, s], lo_[:, s]),
                                        k == 0, k == KD - 1)
                    else:
                        kf = c - 2 * PRODS
                        if kf == 0:
                            pe.wait_ge(m_aux_out, job * JAUX + (AHEAD + PLACE))
                        for h in range(2):
                            s = slice(h * 512, (h + 1) * 512)
                            ins = three(PS[:, 6 + h, :], (GTH[:, kf, :], GTL[:, kf, :]), (hi_[:, s], lo_[:, s]),
                                        kf == 0, kf == KF - 1)
                    ins.then_inc(m_used, 1)
                    for s, what, k in SIDE[c]:
                        bank = 4 + s % 2
                        pe.wait_ge(m_aux_out, job * JAUX + (AHEAD + s - 1))
                        if what == "combine":
                            pe.wait_ge(y_made, job + 1)
                            ins = combine(k, bank)
                        elif what == "turn":
                            pe.wait_ge(prod_made, job * 11 + (k + 1))
                            for m in range(2):
                                ins = M.transpose(PS[:, bank, m * P:(m + 1) * P],
                                                  SG[:, (2 * k + m) * P:(2 * k + m + 1) * P], ident)
                        elif what == "place":
                            pe.wait_ge(sem("pw_made"), job + 1)
                            for t in range(TT):
                                n_ = P if t < 2 else TS
                                ins = M.transpose(PS[:, bank, t * P:t * P + n_], PW[0:n_, t, :],
                                                  CF[0:n_, C_ID:C_ID + n_])
                        else:
                            pe.wait_ge(p_made, job + 2)
                            ins = gather(k, bank)
                        ins.then_inc(m_aux_in, 1)

            with pe.Fori(0, NE) as job:
                job_pe(job)
            pe.wait_ge(sem("routed"), 1)
            extra = pe.value_load(XI[0:1, 4:5], min_val=0, max_val=EXTRA)
            with pe.Fori(0, EXTRA) as k:
                with pe.If(k < extra):
                    job_pe(k + NE)
            pe.wait_ge(y_made, extra + (NE + 1))
            for d in range(KD):
                pe.wait_ge(m_aux_out, extra * JAUX + (NE * JAUX + AHEAD + d - 1))
                combine(d, 4 + d % 2).then_inc(m_aux_in, 1)
            stats()
            pe.wait_ge(x_ready, 4 * KD)
            for k in range(6):
                b = aux()
                n, t0 = (P if k < 4 else TS), P * (k // 2)
                for d in range(4):
                    ins = M.transpose(PS[0:n, b, d * P:(d + 1) * P], X[:, 4 * (k % 2) + d, t0:t0 + n], ident)
                ins.then_inc(aux_in, 1)


INPUTS = ["x_prompt", "x_sample", "c_prompt", "c_sample", "state_hgrn", "w_in", "gm_ln_w", "gm_ln_b", "gm_ws", "gm_bs",
          "hg_lb_raw", "hg_norm_w", "w_branch_a", "w_branch_b", "w_out", "w_ada", "b_ada", "norm_pre_mix",
          "norm_post_mix", "norm_pre_ffn", "norm_post_ffn", "w_ffn_gate", "w_ffn_up", "w_ffn_down", "w_router",
          "b_router", "w_exp_gate", "w_exp_up", "w_exp_down"]
OUTPUTS = {"yp": (1, TP, D), "ys": (NS, LS, D), "sp": (DEPTH, 1, HEADS, P, P), "ss": (DEPTH, NS, HEADS, P, P),
           "v": (DEPTH, NS, LS, D)}


def kernel(**inputs):
    import concourse.bacc as bacc
    from concourse.bass_utils import run_bass_kernel_spmd

    nc = bacc.Bacc("TRN2", target_bir_lowering=False, num_devices=1)
    arrays = {name: np.ascontiguousarray(inputs[name]) for name in INPUTS}
    arrays["const_f"], arrays["const_m"] = constants()
    aps = {name: nc.dram_tensor("in_" + name, v.shape, mybir.dt.from_np(v.dtype), kind="ExternalInput").ap()
           for name, v in arrays.items()}
    outs = {name: nc.dram_tensor("out_" + name, shape, F32, kind="ExternalOutput").ap()
            for name, shape in OUTPUTS.items()}
    build(nc, aps, outs)
    r = run_bass_kernel_spmd(nc, [{"in_" + name: v for name, v in arrays.items()}], core_ids=[0])
    return tuple(r.results[0]["out_" + name] for name in OUTPUTS)
```
